# Optimizing a Trainium2 kernel written in Bass

```python
import math
import jax, jax.numpy as jnp
from jax import lax
import numpy as np

D_MODEL = 1024
BATCH = 1
SEQ = 256
DEPTH = 1

GRID_W = 64
MEM_LEN = 256
MEM_HEADS = 4
MEM_HEAD_DIM = 128
HEAD_DIM = 64
NA_HEADS = 8
NA_WIN_ROWS = 8
NA_WIN_COLS = 16
DIL_GROUPS = ((128, 1), (512, 4), (2048, 16))
DIL_HEADS_PER_GROUP = 4
DIL_HEADS = DIL_HEADS_PER_GROUP * len(DIL_GROUPS)
DIL_BLOCK = 128
T5_BUCKETS = 32
T5_MAX_DIST = 1024
N_EXPERTS = 32
TOP_K = 4
D_FF = D_MODEL
SWIGLU_ALPHA = 1.702
SWIGLU_LIMIT = 7.0
MOE_BLOCK = 128
RMS_EPS = 1e-6
NEG_INF = -1e30

N_BRANCH = 3
WIDTH_A = NA_HEADS * HEAD_DIM
WIDTH_B = DIL_HEADS * HEAD_DIM
WIDTH_B_OUT = DIL_HEADS_PER_GROUP * HEAD_DIM
WIDTH_C = MEM_HEADS * MEM_HEAD_DIM
IN_COLS = 3 * WIDTH_A + 3 * WIDTH_B + WIDTH_C + N_BRANCH * D_MODEL

kernel_name = "hybrid_gated_na_dilated_mem_moe_encoder"

def rms_norm(x, g):
    xf = x.astype(jnp.float32)
    y = xf * lax.rsqrt(jnp.mean(xf * xf, axis=-1, keepdims=True) + RMS_EPS)
    return (y * g.astype(jnp.float32)).astype(x.dtype)

def neighbourhood_attention(q, k, v, rpb):
    B, S, H, dh = q.shape
    rows = S // GRID_W
    wr = min(NA_WIN_ROWS, rows)
    wc = NA_WIN_COLS
    qg = q.reshape(B, rows, GRID_W, H, dh)
    kg = k.reshape(B, rows, GRID_W, H, dh)
    vg = v.reshape(B, rows, GRID_W, H, dh)
    col = jnp.arange(GRID_W)
    col_start = jnp.clip(col - wc // 2, 0, GRID_W - wc)
    col_idx = col_start[:, None] + jnp.arange(wc)[None, :]
    dc = col_idx - col[:, None]
    scale = dh ** -0.5

    def one_row(r):
        rs = jnp.clip(r - wr // 2, 0, rows - wr)
        k_rows = lax.dynamic_slice_in_dim(kg, rs, wr, axis=1)
        v_rows = lax.dynamic_slice_in_dim(vg, rs, wr, axis=1)
        k_win = k_rows[:, :, col_idx]
        v_win = v_rows[:, :, col_idx]
        q_r = lax.dynamic_index_in_dim(qg, r, axis=1, keepdims=False)
        s = jnp.einsum('bqhd,bnqchd->bhqnc', q_r, k_win).astype(jnp.float32) * scale
        dr = rs + jnp.arange(wr) - r
        bias = rpb[:, dr[None, :, None] + NA_WIN_ROWS - 1, dc[:, None, :] + NA_WIN_COLS - 1]
        s = s + bias[None].astype(jnp.float32)
        p = jax.nn.softmax(s.reshape(B, H, GRID_W, wr * wc), axis=-1)
        p = p.reshape(B, H, GRID_W, wr, wc).astype(v.dtype)
        return jnp.einsum('bhqnc,bnqchd->bqhd', p, v_win)

    out = lax.map(one_row, jnp.arange(rows))
    return out.transpose(1, 0, 2, 3, 4).reshape(B, S, H * dh)

def t5_bucket(rel):
    half = T5_BUCKETS // 2
    max_exact = half // 2
    ret = jnp.where(rel > 0, half, 0)
    n = jnp.abs(rel)
    nf = jnp.maximum(n, 1).astype(jnp.float32)
    large = max_exact + (jnp.log(nf / max_exact) / math.log(T5_MAX_DIST / max_exact)
                         * (half - max_exact)).astype(jnp.int32)
    large = jnp.minimum(large, half - 1)
    return ret + jnp.where(n < max_exact, n, large)

def dilated_group_attention(q, k, v, t5_bias, window, dil):
    B, S, H, dh = q.shape
    half = (window // 2) // dil
    L = S // dil
    def split(t):
        return t.reshape(B, L, dil, H, dh).transpose(0, 2, 1, 3, 4)
    qs, ks, vs = split(q), split(k), split(v)
    nb = -(-L // DIL_BLOCK)
    Lp = nb * DIL_BLOCK
    nk = DIL_BLOCK + 2 * half
    qs = jnp.pad(qs, ((0, 0), (0, 0), (0, Lp - L), (0, 0), (0, 0)))
    kp = jnp.pad(ks, ((0, 0), (0, 0), (half, Lp - L + half), (0, 0), (0, 0)))
    vp = jnp.pad(vs, ((0, 0), (0, 0), (half, Lp - L + half), (0, 0), (0, 0)))
    key_idx = jnp.arange(nb)[:, None] * DIL_BLOCK + jnp.arange(nk)[None, :]
    kb = kp[:, :, key_idx]
    vb = vp[:, :, key_idx]
    qb = qs.reshape(B, dil, nb, DIL_BLOCK, H, dh)
    s = jnp.einsum('brnqhd,brnkhd->brnhqk', qb, kb).astype(jnp.float32) * (dh ** -0.5)
    qi = jnp.arange(nb)[:, None] * DIL_BLOCK + jnp.arange(DIL_BLOCK)[None, :]
    ki = key_idx - half
    rel = ki[:, None, :] - qi[:, :, None]
    valid = (jnp.abs(rel) <= half) & (ki[:, None, :] >= 0) & (ki[:, None, :] < L)
    bias = t5_bias[t5_bucket(rel * dil)].astype(jnp.float32)
    s = s + bias.transpose(0, 3, 1, 2)[None, None]
    s = jnp.where(valid[None, None, :, None], s, NEG_INF)
    lse = jax.nn.logsumexp(s, axis=-1)
    p = jnp.exp(s - lse[..., None]).astype(v.dtype)
    o = jnp.einsum('brnhqk,brnkhd->brnqhd', p, vb)
    o = o.reshape(B, dil, Lp, H, dh)[:, :, :L].transpose(0, 2, 1, 3, 4).reshape(B, S, H, dh)
    lse = lse.transpose(0, 1, 2, 4, 3).reshape(B, dil, Lp, H)[:, :, :L]
    lse = lse.transpose(0, 2, 1, 3).reshape(B, S, H)
    return o, lse

def dilated_mixture(q, k, v, t5_bias):
    B, S, _, dh = q.shape
    G = DIL_HEADS_PER_GROUP
    outs, lses = [], []
    for gi, (window, dil) in enumerate(DIL_GROUPS):
        sl = slice(gi * G, (gi + 1) * G)
        o, l = dilated_group_attention(q[:, :, sl], k[:, :, sl], v[:, :, sl],
                                       t5_bias[:, sl], window, dil)
        outs.append(o)
        lses.append(l)
    w = jax.nn.softmax(jnp.stack(lses, axis=0), axis=0).astype(q.dtype)
    o = jnp.sum(w[..., None] * jnp.stack(outs, axis=0), axis=0)
    return o.reshape(B, S, G * dh)

def memory_attention(q, mk, mv):
    B, S, H, dh = q.shape
    s = jnp.einsum('bshd,bmhd->bhsm', q, mk).astype(jnp.float32) * (dh ** -0.5)
    p = jax.nn.softmax(s, axis=-1).astype(mv.dtype)
    return jnp.einsum('bhsm,bmhd->bshd', p, mv).reshape(B, S, H * dh)

def moe_ffn(h, router_w, router_b, w_gu, b_gu, w_dn, b_dn):
    N, D = h.shape
    logits = (h @ router_w).astype(jnp.float32) + router_b.astype(jnp.float32)
    top_val, top_idx = lax.top_k(logits, TOP_K)
    top_w = jax.nn.softmax(top_val, axis=-1)
    A = N * TOP_K
    e_flat = top_idx.reshape(-1)
    tok_flat = jnp.repeat(jnp.arange(N, dtype=jnp.int32), TOP_K)
    w_flat = top_w.reshape(-1)
    order = jnp.argsort(e_flat)
    e_sorted = e_flat[order]
    counts = jnp.bincount(e_flat, length=N_EXPERTS)
    starts = jnp.cumsum(counts) - counts
    padded = (counts + MOE_BLOCK - 1) // MOE_BLOCK * MOE_BLOCK
    pad_ends = jnp.cumsum(padded)
    pad_starts = pad_ends - padded
    dest = pad_starts[e_sorted] + (jnp.arange(A) - starts[e_sorted])
    n_slots = (-(-A // MOE_BLOCK)) * MOE_BLOCK + N_EXPERTS * MOE_BLOCK
    n_blocks = n_slots // MOE_BLOCK
    slot_tok = jnp.zeros((n_slots,), jnp.int32).at[dest].set(tok_flat[order])
    slot_w = jnp.zeros((n_slots,), h.dtype).at[dest].set(w_flat[order].astype(h.dtype))
    block_expert = jnp.minimum(
        jnp.searchsorted(pad_ends, jnp.arange(n_blocks) * MOE_BLOCK, side='right'), N_EXPERTS - 1)
    xs = h[slot_tok].reshape(n_blocks, MOE_BLOCK, D)

    def expert_block(args):
        xb, e = args
        gu = xb @ w_gu[e] + b_gu[e]
        g = jnp.minimum(gu[:, :D_FF], SWIGLU_LIMIT)
        u = jnp.clip(gu[:, D_FF:], -SWIGLU_LIMIT, SWIGLU_LIMIT)
        a = (u + 1.0) * (g * jax.nn.sigmoid(SWIGLU_ALPHA * g))
        return a @ w_dn[e] + b_dn[e]

    ys = lax.map(expert_block, (xs, block_expert)).reshape(n_slots, D)
    return jnp.zeros_like(h).at[slot_tok].add(ys * slot_w[:, None])

def setup_inputs(seed: int = 0) -> dict:
    key = jax.random.key(seed)
    ks = jax.random.split(key, 24)
    f32 = jnp.float32
    nrm = lambda k, shape, s: jax.random.normal(k, shape, f32) * s
    L = DEPTH
    return {
        "x": nrm(ks[0], (BATCH, SEQ, D_MODEL), 1.0),
        "mem": nrm(ks[1], (BATCH, MEM_LEN, D_MODEL), 1.0),
        "attn_norm_g": 1.0 + nrm(ks[2], (L, D_MODEL), 0.02),
        "mem_norm_g": 1.0 + nrm(ks[3], (L, D_MODEL), 0.02),
        "w_in": nrm(ks[4], (L, D_MODEL, IN_COLS), D_MODEL ** -0.5),
        "w_mem_kv": nrm(ks[5], (L, D_MODEL, 2 * WIDTH_C), D_MODEL ** -0.5),
        "na_rpb": nrm(ks[6], (L, NA_HEADS, 2 * NA_WIN_ROWS - 1, 2 * NA_WIN_COLS - 1), 0.2),
        "t5_rel_bias": nrm(ks[7], (T5_BUCKETS, DIL_HEADS), 0.2),
        "w_branch_a": nrm(ks[8], (L, WIDTH_A, D_MODEL), WIDTH_A ** -0.5),
        "w_branch_b": nrm(ks[9], (L, WIDTH_B_OUT, D_MODEL), WIDTH_B_OUT ** -0.5),
        "w_branch_c": nrm(ks[10], (L, WIDTH_C, D_MODEL), WIDTH_C ** -0.5),
        "w_out": nrm(ks[11], (L, D_MODEL, D_MODEL), D_MODEL ** -0.5),
        "ffn_norm_g": 1.0 + nrm(ks[12], (L, D_MODEL), 0.02),
        "router_w": nrm(ks[13], (L, D_MODEL, N_EXPERTS), D_MODEL ** -0.5),
        "router_b": nrm(ks[14], (L, N_EXPERTS), 0.01),
        "expert_w_gate_up": nrm(ks[15], (L, N_EXPERTS, D_MODEL, 2 * D_FF), D_MODEL ** -0.5),
        "expert_b_gate_up": nrm(ks[16], (L, N_EXPERTS, 2 * D_FF), 0.02),
        "expert_w_down": nrm(ks[17], (L, N_EXPERTS, D_FF, D_MODEL), D_FF ** -0.5),
        "expert_b_down": nrm(ks[18], (L, N_EXPERTS, D_MODEL), 0.02),
        "final_norm_g": 1.0 + nrm(ks[19], (D_MODEL,), 0.02),
    }

def reference(x, mem, attn_norm_g, mem_norm_g, w_in, w_mem_kv, na_rpb, t5_rel_bias,
              w_branch_a, w_branch_b, w_branch_c, w_out, ffn_norm_g, router_w, router_b,
              expert_w_gate_up, expert_b_gate_up, expert_w_down, expert_b_down, final_norm_g):
    B, S, D = x.shape
    M = mem.shape[1]
    split_points = list(np.cumsum([WIDTH_A, WIDTH_A, WIDTH_A, WIDTH_B, WIDTH_B, WIDTH_B, WIDTH_C])[:])
    for l in range(DEPTH):
        h = rms_norm(x, attn_norm_g[l])
        proj = h @ w_in[l]
        qa, ka, va, qb, kb, vb, qc, gate_logits = jnp.split(proj, split_points, axis=-1)
        qa = qa.reshape(B, S, NA_HEADS, HEAD_DIM)
        ka = ka.reshape(B, S, NA_HEADS, HEAD_DIM)
        va = va.reshape(B, S, NA_HEADS, HEAD_DIM)
        qb = qb.reshape(B, S, DIL_HEADS, HEAD_DIM)
        kb = kb.reshape(B, S, DIL_HEADS, HEAD_DIM)
        vb = vb.reshape(B, S, DIL_HEADS, HEAD_DIM)
        qc = qc.reshape(B, S, MEM_HEADS, MEM_HEAD_DIM)
        gates = jax.nn.sigmoid(gate_logits.astype(jnp.float32)).astype(x.dtype)
        gates = gates.reshape(B, S, N_BRANCH, D)

        m = rms_norm(mem, mem_norm_g[l])
        mk, mv = jnp.split(m @ w_mem_kv[l], 2, axis=-1)
        mk = mk.reshape(B, M, MEM_HEADS, MEM_HEAD_DIM)
        mv = mv.reshape(B, M, MEM_HEADS, MEM_HEAD_DIM)

        y_a = neighbourhood_attention(qa, ka, va, na_rpb[l]) @ w_branch_a[l]
        y_b = dilated_mixture(qb, kb, vb, t5_rel_bias) @ w_branch_b[l]
        y_c = memory_attention(qc, mk, mv) @ w_branch_c[l]
        merged = gates[:, :, 0] * y_a + gates[:, :, 1] * y_b + gates[:, :, 2] * y_c
        x = x + merged @ w_out[l]

        h = rms_norm(x, ffn_norm_g[l])
        y = moe_ffn(h.reshape(B * S, D), router_w[l], router_b[l], expert_w_gate_up[l],
                    expert_b_gate_up[l], expert_w_down[l], expert_b_down[l])
        x = x + y.reshape(B, S, D)
    return rms_norm(x, final_norm_g)


_drawn_inputs = setup_inputs


def setup_inputs(seed=0):
    import zlib

    import numpy as np

    out = dict(_drawn_inputs(seed))
    spreads = {}
    factors = {'mem_norm_g': 5.021,
     'expert_b_gate_up': 5.124,
     'expert_b_down': 5.932,
     'final_norm_g': 8.055,
     'na_rpb': 2.867,
     't5_rel_bias': 6.426,
     'router_b': 3.416}
    for name, (base, spread) in spreads.items():
        noise = np.random.default_rng([zlib.crc32(name.encode()), seed]).standard_normal(out[name].shape)
        drawn = base * np.exp(spread * noise) if base else spread * noise
        out[name] = __import__('jax').numpy.asarray(drawn.astype(out[name].dtype))
    for name, factor in factors.items():
        out[name] = (out[name] * factor).astype(out[name].dtype)
    return out
```

```python
import math
from contextlib import ExitStack

import numpy as np
import concourse.bass as bass
from concourse import mybir

F32 = mybir.dt.float32
I32 = mybir.dt.int32
ALU = mybir.AluOpType
ACT = mybir.ActivationFunctionType
AX_X = mybir.AxisListType.X

P = 128
D = 1024
KC = D // P
S = 256
T = S // P
MEM = 256
GRID_W, WIN_COLS, WIN_ROWS = 64, 16, 8
NA_HEADS, HD = 8, 64
DIL = (1, 4, 16)
DIL_WINDOW = (128, 512, 2048)
GROUP_HEADS = 4
DIL_HEADS = GROUP_HEADS * len(DIL)
MEM_HEADS, MEM_HD = 4, 128
T5_BUCKETS, T5_MAX_DIST = 32, 1024
EXPERTS, TOP_K = 32, 4
ALPHA, LIMIT, EPS = 1.702, 7.0, 1e-6
NEG = -1e30
SENTINEL = -3e38
REPLACED = -3.2e38
NO_SLOT = 4096.0

BLK = 64
CHUNK = 2048
RING = 12
FRONT_RING = 10
EXPERT_CHUNKS = 12
MAX_OVERFLOW = S * TOP_K // BLK
REL = 2 * S
IMG = 3 * P
SLOTS_W = 256

FRONT = ([("mem", i) for i in range(4)] + [("in", i) for i in (15, 16)] + [("in", i) for i in range(15)]
         + [("in", i) for i in range(17, 21)] + [("branch_a", 0), ("branch_a", 1)]
         + [("in", i) for i in range(25, 29)] + [("branch_c", 0), ("branch_c", 1)]
         + [("in", i) for i in range(21, 25)] + [("branch_b", 0)] + [("out", i) for i in range(4)])
NF = len(FRONT)
OUT0 = NF - 4
UNITS = [("C", 0, 0), ("C", 1, 0)] + [("A", j, 0) for j in range(4)] + [("B", j, g) for j in range(2) for g in range(3)]
NU = len(UNITS)
OUTPUT_OF = [0, 1, 2, 3, 4, 5, 6, 6, 6, 7, 7, 7]
TURN_LAG, PV_LAG = 3, 4
STEP_AFTER = {6: 0, 7: 1, 11: 2, 12: 3, 13: 4, 14: 5, 20: 6, 21: 7, 22: 8, 23: 9, 24: 10, 27: 11, 28: 12, 29: 13,
              30: 14, 31: 15}
QKT = {0: 0, 1: 2, 2: 4, 3: 6, 6: 8, 7: 10, 8: 12, 9: 14, 10: 16, 11: 18, 15: 20, 16: 22}
V_COL = {4: 0, 5: 256, 12: 512, 13: 768, 14: 1024}
Q_SCALE = {0: HD ** -0.5, 1: HD ** -0.5, 6: HD ** -0.5, 7: HD ** -0.5, 8: HD ** -0.5,
           15: MEM_HD ** -0.5, 16: MEM_HD ** -0.5}
GATE_BRANCH = {**{i: (0, i - 17) for i in range(17, 21)}, **{i: (1, i - 25) for i in range(25, 29)},
               **{i: (0, i - 21) for i in range(21, 25)}}


def image_rows(u):
    kind, j, g = UNITS[u]
    return 2 * j if kind == "A" else NA_HEADS + g * GROUP_HEADS + 2 * j


def unit_blocks(u):
    kind, j, g = UNITS[u]
    if kind == "A":
        return j, 4 + j, 128 * j
    b = g * 2 + j
    return 8 + b, 14 + b, 512 + 128 * b


def last_unit_of(o):
    return max(u for u in range(NU) if OUTPUT_OF[u] == o)


def build(nc, t):
    w_in = t["w_in"].rearrange("l (k p) c -> (l p) k c", p=P)
    w_mem = t["w_mem_kv"].rearrange("l (k p) c -> (l p) k c", p=P)
    w_out = t["w_out"].rearrange("l (k p) c -> (l p) k c", p=P)
    w_br = {b: t[f"w_{b}"].rearrange("l (k p) c -> (l p) k c", p=P) for b in ("branch_a", "branch_b", "branch_c")}
    w_gu = t["expert_w_gate_up"].rearrange("l e (k p) c -> (l e) p k c", p=P)
    w_dn = t["expert_w_down"].rearrange("l e (k p) c -> (l e) p k c", p=P)
    b_gu = t["expert_b_gate_up"]
    na_rows = t["na_rows"]
    t5_scratch = nc.dram_tensor("t5_scratch", [DIL_HEADS, REL], F32, kind="Internal").ap()

    with ExitStack() as ctx:
        def sb(name, shape, dt=F32):
            return ctx.enter_context(nc.sbuf_tensor(name, shape, dt))

        def sem(name):
            return ctx.enter_context(nc.semaphore(name))

        ring = sb("ring", [P, RING, CHUNK])
        ident = sb("ident", [P, P])
        earlier = sb("earlier", [P, P])
        ones = sb("ones", [P, P])
        na_mask = sb("na_mask", [P, GRID_W])
        g_rows = sb("g_rows", [3 * KC, P])
        g_cols = sb("g_cols", [P, 4 * KC])
        eps = sb("eps", [P, 1])
        x = sb("x_tokens", [P, T, D])
        xn = sb("x_normed", [P, T, D])
        hT = sb("h_T", [P, KC, S])
        rw = sb("router_w_sb", [P, KC, EXPERTS])
        rb = sb("router_b_sb", [P, EXPERTS])
        sumsq = sb("sumsq", [P, 4, T])
        rstd = sb("rstd", [P, 4, T])
        onehot = sb("onehot", [T5_BUCKETS + 3, REL])
        t5_in = sb("t5_in", [T5_BUCKETS + 3, DIL_HEADS])
        row_max = sb("row_max", [P, NU, 4])
        neg_max = sb("neg_max", [P, 8, 4])
        exp_sum = sb("exp_sum", [P, NU, 4])
        inv_sum = sb("inv_sum", [P, 8, 4])
        b_tmp = sb("b_tmp", [P, 2, 4])
        WORK = 20480
        work = sb("work", [P, WORK])

        def area(off, *dims):
            n = int(np.prod(dims))
            assert off + n <= WORK
            flat = work[:, off:off + n]
            if len(dims) == 2:
                return flat.rearrange("p (a b) -> p a b", a=dims[0])
            if len(dims) == 3:
                return flat.rearrange("p (a b c) -> p a b c", a=dims[0], b=dims[1])
            if len(dims) == 4:
                return flat.rearrange("p (a b c d) -> p a b c d", a=dims[0], b=dims[1], c=dims[2])
            return flat

        image = area(0, 4, 2, IMG)
        pT = area(3072, 2, 2, 2, S)
        qkT = area(5120, 24, S)
        v = area(11264, T, 1280)
        mkT = area(13824, MEM_HEADS, MEM)
        mv = area(14848, T, MEM_HEADS * MEM_HD)
        gates = area(15872, 2, T, D)
        mem_raw = area(3072, T, D)
        mem_n = area(15872, T, D)
        mT = area(15872 + 2048, KC, MEM)
        t5_rows = area(5120, REL)[0:DIL_HEADS, :]
        scores = ring[:, FRONT_RING:, :].rearrange("p a (b h t k) -> p (a b) h t k", b=2, h=2, t=2)
        brow = area(0, 2, 2 * D)
        XT = area(4096, 2, KC, 2 * BLK)
        P_pair = area(6144, T, 2 * BLK)
        PW = area(6400, T, 2 * BLK)
        WT = area(6656, 2, S)
        gate_c = area(7168, 512)
        up_c = area(7680, 512)
        sig = area(8192, 512)
        gu_prod = area(8704, 512)
        act_out = area(9216, 512)
        aT = area(9728, 4, P)
        y_sb = area(10240, 512)
        b_dn = area(10752, D)[0:EXPERTS, :]
        final_g = area(11776, D)
        iota = area(12800, D)
        logits = area(13824, T, 40)
        top8 = area(13904, T, 8)
        replaced = area(13920, T, 40)
        mask = area(14000, T, EXPERTS)
        neg_top = area(14064, T)
        prob = area(14066, T, EXPERTS)
        prob_m = area(14130, T, EXPERTS)
        w_sum = area(14194, T)
        w_inv = area(14196, T)
        w_sel = area(14198, T, EXPERTS)
        keys = area(14262, T, EXPERTS + 4)
        okeys = area(14334, T, EXPERTS)
        count = area(14398, EXPERTS)
        extra = area(14430, EXPERTS)
        ends = area(14462, EXPERTS)
        tmp_a = area(14494, T, EXPERTS)
        tmp_b = area(14558, T, EXPERTS)
        ends_le = area(14622, MAX_OVERFLOW, EXPERTS)
        ovf_f = area(15134, MAX_OVERFLOW)
        wT_sel = area(15150, S)[0:EXPERTS, :]
        final = area(15406, T, D)
        ovf = sb("ovf", [P, MAX_OVERFLOW + 1], I32)

        ps = ctx.enter_context(nc.psum_tensor("ps", [P, 8, 512], F32))

        landed = [sem(f"landed{i}") for i in range(RING)]
        consts_in = sem("consts_in")
        mem_in = sem("mem_in")
        x_in = sem("x_in")
        t5_saved = sem("t5_saved")
        image_in = [sem(f"image_in{i}") for i in range(4)]
        late_in = sem("late_in")
        brow_in = [sem(f"brow_in{i}") for i in range(2)]
        out_saved = sem("out_saved")
        chunk_used = sem("chunk_used")
        gcols_ps, gcols_ok = sem("gcols_ps"), sem("gcols_ok")
        t5_ps, t5_copied = sem("t5_ps"), sem("t5_copied")
        normed = sem("normed")
        turned = sem("turned")
        hT_act, hT_dve = sem("hT_act"), sem("hT_dve")
        sq_done, std_ready = sem("sq_done"), sem("std_ready")
        probs_exp = sem("probs_exp")
        front_evac = sem("front_evac")
        scores_ready, scores_drained = sem("scores_ready"), sem("scores_drained")
        max_ready, exp_done, probs_ready = sem("max_ready"), sem("exp_done"), sem("probs_ready")
        probs_turned, pT_dve, pT_act = sem("probs_turned"), sem("pT_dve"), sem("pT_act")
        pv_done, out_evac = sem("pv_done"), sem("out_evac")
        merged_ready = sem("merged_ready")
        x1_ready = sem("x1_ready")
        router_ps, top_ready = sem("router_ps"), sem("top_ready")
        mask_ready, rank_ps, wsel_ready = sem("mask_ready"), sem("rank_ps"), sem("wsel_ready")
        wT_ps, wT_ok = sem("wT_ps"), sem("wT_ok")
        routed = sem("routed")
        P_ready, gathered, XT_ready = sem("P_ready"), sem("gathered"), sem("XT_ready")
        PW_ready, WT_ps, WT_ready = sem("PW_ready"), sem("WT_ps"), sem("WT_ready")
        gate_ready, gu_drained, sig_ready = sem("gate_ready"), sem("gu_drained"), sem("sig_ready")
        prod_ready, act_ready = sem("prod_ready"), sem("act_ready")
        aT_ps, aT_ready, y_ready, scattered = sem("aT_ps"), sem("aT_ready"), sem("y_ready"), sem("scattered")
        final_ready = sem("final_ready")
        dve_chain = sem("dve_chain")
        eps_ready = sem("eps_ready")

        block = ctx.enter_context(nc.Block())

        def front_landed(eng, i):
            eng.wait_ge(landed[i % FRONT_RING], 16 * (i // FRONT_RING + 1))

        def ring_slot(j):
            return (j + NF % FRONT_RING) % RING

        def front_fills(r):
            return len(range(r, NF, FRONT_RING)) if r < FRONT_RING else 0


        def bcast(ap, axis, n):
            dims = [list(d) for d in ap.ap]
            return bass.AP(ap.tensor, ap.offset, dims[:axis] + [[0, n]] + dims[axis:])

        def reversed_tiles(ap):
            dims = [list(d) for d in ap.ap]
            step, n = dims[-1]
            return bass.AP(ap.tensor, ap.offset + (P - 1) * step, dims[:-1] + [[P * step, n // P], [-step, P]])

        @block.sync
        def _(sp):
            sp.dma_start(mem_raw, t["mem"].rearrange("b (t p) d -> (b p) t d", p=P)).then_inc(mem_in, 16)
            for i in range(NF):
                if i == 1:
                    sp.dma_start(x[:], t["x"].rearrange("b (t p) d -> (b p) t d", p=P)).then_inc(x_in, 16)
                if i >= FRONT_RING:
                    sp.wait_ge(chunk_used, i - FRONT_RING + 1)
                kind, n = FRONT[i]
                dst = ring[:, i % FRONT_RING, :]
                if kind in ("mem", "in", "out"):
                    src = {"mem": w_mem, "in": w_in, "out": w_out}[kind][:, :, n * SLOTS_W:(n + 1) * SLOTS_W]
                    dst = dst.rearrange("p (k c) -> p k c", k=KC)
                elif kind == "branch_b":
                    src, dst = w_br[kind], dst.rearrange("p (k c) -> p k c", k=2)
                else:
                    src, dst = w_br[kind][:, :, n * 512:(n + 1) * 512], dst.rearrange("p (k c) -> p k c", k=4)
                sp.dma_start(dst, src).then_inc(landed[i % FRONT_RING], 16)

            def load_expert(e, n, bias_slot, first=False):
                for j in range(EXPERT_CHUNKS):
                    r = ring_slot(j)
                    if first and 0 < front_fills(r):
                        sp.wait_ge(chunk_used, max(i for i in range(NF) if i % FRONT_RING == r) + 1)
                    elif not first:
                        sp.wait_ge(chunk_used, NF + EXPERT_CHUNKS * (n - 1) + j + 1)
                    if j == 0:
                        sp.dma_start(brow[0:1, bias_slot, :], b_gu[0, bass.ds(e, 1), :]).then_inc(brow_in[bias_slot], 16)
                    if j < KC:
                        src = w_gu[bass.ds(e, 1), :, j, :].rearrange("o p c -> (o p) c")
                        dst = ring[:, r, :]
                    else:
                        src = w_dn[bass.ds(e, 1), :, 2 * (j - KC):2 * (j - KC) + 2, :].rearrange("o p k c -> (o p) k c")
                        dst = ring[:, r, :].rearrange("p (k c) -> p k c", k=2)
                    sp.dma_start(dst, src).then_inc(landed[r], 16)

            sp.wait_ge(pv_done, NU)
            for e in range(4):
                load_expert(e, e, e % 2, first=e == 0)
            with sp.Fori(1, EXPERTS // 4) as it:
                for q in range(4):
                    load_expert(it * 4 + q, it * 4 + q, q % 2)
            sp.wait_ge(routed, 1)
            n_over = sp.value_load(ovf[0:1, MAX_OVERFLOW:MAX_OVERFLOW + 1], min_val=0, max_val=MAX_OVERFLOW)
            with sp.If(0 < n_over):
                with sp.Fori(0, MAX_OVERFLOW) as b:
                    with sp.If(b < n_over):
                        e_b = sp.value_load(ovf[0:1, bass.ds(b, 1)], min_val=0, max_val=EXPERTS - 1)
                        load_expert(e_b, b + EXPERTS, 0)
            sp.wait_ge(final_ready, 1)
            sp.dma_start(t["out"].rearrange("b (t p) d -> (b p) t d", p=P), final).then_inc(out_saved, 16)
            sp.wait_ge(out_saved, 16)

        @block.gpsimd
        def _(pool):
            pool.dma_start(g_rows[:], t["g_rows"]).then_inc(consts_in, 16)
            pool.dma_start(ident[:], t["ident"]).then_inc(consts_in, 16)
            pool.dma_start(t5_in[0:T5_BUCKETS, :], t["t5_rel_bias"]).then_inc(consts_in, 16)
            pool.dma_start(t5_in[T5_BUCKETS:T5_BUCKETS + 3, :], t["group_of_head"]).then_inc(consts_in, 16)
            pool.dma_start(onehot[:], t["bucket_onehot"]).then_inc(consts_in, 16)
            pool.dma_start(na_mask[:], t["na_mask"]).then_inc(consts_in, 16)
            pool.dma_start(earlier[:], t["earlier"]).then_inc(consts_in, 16)
            pool.dma_start(rw[:], t["router_w"].rearrange("l (k p) e -> (l p) k e", p=P)).then_inc(consts_in, 16)
            pool.dma_start(rb[:], t["router_b"].partition_broadcast(P).rearrange("p l e -> p (l e)")
                           if False else bass.AP(t["router_b"].tensor, 0, [[0, P], [1, EXPERTS]])).then_inc(consts_in, 16)
            pool.wait_ge(t5_copied, 1)
            pool.dma_start(t5_scratch, t5_rows).then_inc(t5_saved, 16)
            pool.wait_ge(t5_saved, 16)
            for u in range(2, NU):
                i = u - 2
                if i >= 4:
                    pool.wait_ge(scores_drained, u - 3)
                row = image_rows(u)
                rows, row = (na_rows, row) if row < NA_HEADS else (t5_scratch, row - NA_HEADS)
                pool.dma_start(image[:, i % 4], bass.AP(rows.tensor, row * REL, [[1, P], [REL, 2], [1, IMG]])
                               ).then_inc(image_in[i % 4], 16)
            pool.wait_ge(merged_ready, 2)
            pool.wait_ge(chunk_used, OUT0)
            pool.dma_start(b_dn, t["expert_b_down"].rearrange("l e c -> (l e) c")).then_inc(late_in, 16)
            pool.dma_start(final_g, bass.AP(t["final_norm_g"].tensor, 0, [[0, P], [1, D]])).then_inc(late_in, 16)
            pool.dma_start(iota, bass.AP(t["iota"].tensor, 0, [[0, P], [1, D]])).then_inc(late_in, 16)

        @block.tensor
        def _(pe):
            def mm(out, lhsT, rhs, start, stop, **kw):
                return nc.tensor.matmul(out, lhsT, rhs, start=start, stop=stop, **kw)

            def turn(src, m, first_bank):
                pe.wait_ge(normed, m + 1)
                for k in range(KC):
                    for tt in range(T):
                        last = nc.tensor.transpose(ps[:, first_bank + k // 2, (k % 2) * S + tt * P:(k % 2) * S + (tt + 1) * P],
                                                   src[:, tt, k * P:(k + 1) * P], ident[:])
                    if k % 2:
                        last.then_inc(turned, 1)

            pe.wait_ge(consts_in, 16 * 9)
            nc.tensor.transpose(ps[:, 6, 0:3 * KC], g_rows[:], ident[0:3 * KC, 0:3 * KC]).then_inc(gcols_ps, 1)
            mm(ps[0:DIL_HEADS, 7, :], t5_in[:], onehot[:], True, True).then_inc(t5_ps, 1)
            turn(mem_n, 0, 0)
            pe.wait_ge(gcols_ok, 1)
            pe.wait_ge(t5_copied, 1)
            turn(xn, 1, 4)

            def head_scores(u):
                kind, j, g = UNITS[u]
                pe.wait_ge(front_evac, {"C": 6, "A": 12, "B": 21}[kind])
                if u:
                    pe.wait_ge(scores_drained, u)
                else:
                    pe.wait_ge(hT_act, 8)
                    pe.wait_ge(hT_dve, 8)
                for tt in range(T):
                    for hh in range(2):
                        out = ps[:, 2 + hh, tt * S:(tt + 1) * S]
                        if kind == "C":
                            h = 2 * j + hh
                            last = mm(out, qkT[:, 20 + h, tt * P:(tt + 1) * P], mkT[:, h, :], True, True)
                        else:
                            qb, kb, _ = unit_blocks(u)
                            rows = slice(64 * hh, 64 * hh + 64)
                            last = mm(out, qkT[rows, qb, tt * P:(tt + 1) * P], qkT[rows, kb, :], True, True)
                last.then_inc(scores_ready, 1)

            def turn_probs(u):
                pe.wait_ge(probs_ready, u + 1)
                if u:
                    pe.wait_ge(pT_dve, u)
                    pe.wait_ge(pT_act, u)
                for hh in range(2):
                    for kt in range(T):
                        for tt in range(T):
                            last = nc.tensor.transpose(ps[:, 6 + hh, kt * S + tt * P:kt * S + (tt + 1) * P],
                                                       scores[:, u % 4, hh, tt, kt * P:(kt + 1) * P], ident[:])
                last.then_inc(probs_turned, 1)

            def attend(u):
                kind, j, g = UNITS[u]
                o = OUTPUT_OF[u]
                pe.wait_ge(pT_dve, u + 1)
                pe.wait_ge(pT_act, u + 1)
                if o >= 2:
                    pe.wait_ge(out_evac, o - 1)
                for kt in range(T):
                    for hh in range(2):
                        rhs = pT[:, u % 2, hh, kt, :]
                        if kind == "C":
                            continue
                        _, _, vc = unit_blocks(u)
                        last = mm(ps[64 * hh:64 * hh + 64, 4 + o % 2, 0:S], v[:, kt, vc + 64 * hh:vc + 64 * hh + 64], rhs,
                                  kt == 0 and g == 0, kt == T - 1 and (kind == "A" or g == 2))
                if kind == "C":
                    for hh in range(2):
                        for kt in range(T):
                            h = 2 * j + hh
                            last = mm(ps[:, 4 + o % 2, hh * S:(hh + 1) * S], mv[:, kt, h * P:(h + 1) * P],
                                      pT[:, u % 2, hh, kt, :], kt == 0, kt == T - 1)
                last.then_inc(pv_done, 1)

            for i, (kind, n) in enumerate(FRONT):
                if i == 0:
                    pe.wait_ge(hT_act, 4)
                    pe.wait_ge(hT_dve, 4)
                if i == 4:
                    pe.wait_ge(hT_act, 8)
                    pe.wait_ge(hT_dve, 8)
                front_landed(pe, i)
                chunk = ring[:, i % FRONT_RING, :]
                prev_y = i and FRONT[i - 1][0].startswith("branch")
                if kind in ("mem", "in"):
                    if i >= 2:
                        pe.wait_ge(front_evac, i if prev_y else i - 1)
                    chunk = chunk.rearrange("p (k c) -> p k c", k=KC)
                    src = mT if kind == "mem" else hT
                    if (kind == "mem" and n < 2) or (kind == "in" and n in QKT):
                        for b in range(2):
                            for k in range(KC):
                                last = mm(ps[:, i % 2, b * S:(b + 1) * S], chunk[:, k, b * P:(b + 1) * P], src[:, k, :],
                                          k == 0, k == KC - 1)
                    else:
                        for tt in range(T):
                            for k in range(KC):
                                last = mm(ps[:, i % 2, tt * S:(tt + 1) * S], src[:, k, tt * P:(tt + 1) * P], chunk[:, k, :],
                                          k == 0, k == KC - 1)
                elif kind == "out":
                    if i == OUT0:
                        pe.wait_ge(hT_act, 12)
                        pe.wait_ge(hT_dve, 12)
                    pe.wait_ge(front_evac, i if prev_y else i - 1)
                    chunk = chunk.rearrange("p (k c) -> p k c", k=KC)
                    for tt in range(T):
                        for k in range(KC):
                            last = mm(ps[:, i % 2, tt * S:(tt + 1) * S], hT[:, k, tt * P:(tt + 1) * P], chunk[:, k, :],
                                      k == 0, k == KC - 1)
                else:
                    pe.wait_ge(front_evac, i)
                    pe.wait_ge(out_evac, {"branch_a": 6, "branch_c": 2, "branch_b": 8}[kind])
                    first = {"branch_a": 0, "branch_c": 20, "branch_b": 8}[kind]
                    halves, kc = (2, 2) if kind == "branch_b" else (1, 4)
                    chunk = chunk.rearrange("p (k h c) -> p k h c", k=kc, h=halves)
                    for half in range(halves):
                        for tt in range(T):
                            for k in range(kc):
                                last = mm(ps[:, 2 * half + tt, :], qkT[:, first + k, tt * P:(tt + 1) * P],
                                          chunk[:, k, half, :], k == 0, k == kc - 1)
                last.then_inc(chunk_used, 1)
                if i in STEP_AFTER:
                    s = STEP_AFTER[i]
                    if s < NU:
                        head_scores(s)
                    if 0 <= s - TURN_LAG < NU:
                        turn_probs(s - TURN_LAG)
                    if 0 <= s - PV_LAG < NU:
                        attend(s - PV_LAG)
                if kind == "branch_b":
                    for half in range(2):
                        pe.wait_ge(merged_ready, half + 1)
                        for k in range(4 * half, 4 * half + 4):
                            for tt in range(T):
                                last = nc.tensor.transpose(ps[:, 4 + k // 2, (k % 2) * S + tt * P:(k % 2) * S + (tt + 1) * P],
                                                           xn[:, tt, k * P:(k + 1) * P], ident[:])
                            if k % 2:
                                last.then_inc(turned, 1)

            turn(xn, 2, 2)
            pe.wait_ge(hT_act, 16)
            pe.wait_ge(hT_dve, 16)
            for tt in range(T):
                for k in range(KC):
                    last = mm(ps[:, 6, tt * EXPERTS:(tt + 1) * EXPERTS], hT[:, k, tt * P:(tt + 1) * P], rw[:, k, :],
                              k == 0, k == KC - 1)
            last.then_inc(router_ps, 1)
            pe.wait_ge(mask_ready, 1)
            mm(ps[:, 7, 0:EXPERTS], earlier[:], mask[:, 0, :], True, True)
            mm(ps[:, 7, 32:32 + EXPERTS], ones[:], mask[:, 0, :], True, False)
            mm(ps[:, 7, 32:32 + EXPERTS], earlier[:], mask[:, 1, :], False, True)
            mm(ps[:, 7, 64:64 + EXPERTS], ones[:], mask[:, 0, :], True, False)
            mm(ps[:, 7, 64:64 + EXPERTS], ones[:], mask[:, 1, :], False, True).then_inc(rank_ps, 1)
            pe.wait_ge(wsel_ready, 1)
            for tt in range(T):
                last = nc.tensor.transpose(ps[0:EXPERTS, 1, tt * P:(tt + 1) * P], w_sel[:, tt, :], ident[:])
            last.then_inc(wT_ps, 1)

            def gather_half(half, width):
                for k in range(4):
                    for tt in range(T):
                        last = mm(ps[:, 3, k * P:k * P + width], xn[:, tt, (4 * half + k) * P:(4 * half + k + 1) * P],
                                  P_pair[:, tt, 0:width], tt == 0, tt == T - 1)
                last.then_inc(gathered, 1)

            def scatter():
                for tt in range(T):
                    for hn in range(2):
                        last = mm(ps[:, 4 + 2 * tt + hn, :], WT_of[0][64 * hn:64 * hn + 64, tt * P:(tt + 1) * P],
                                  y_sb[64 * hn:64 * hn + 64, :], False, False, skip_group_check=True)
                last.then_inc(scattered, 1)

            WT_of = [WT[:, 1, :]]

            def expert(n, wt_slot, bias_slot, bias_fill, xt, xt_fill, gather):
                def chunk_landed(j):
                    pe.wait_ge(landed[ring_slot(j)], (n + 1 + front_fills(ring_slot(j))) * 16)

                pe.wait_ge(brow_in[bias_slot], bias_fill)
                pe.wait_ge(gu_drained, n + 1)
                for b in range(2):
                    for h in range(2):
                        mm(ps[64 * h:64 * h + 64, b, :], ones[0:1, 0:BLK],
                           brow[0:1, bias_slot, b * D + 512 * h:b * D + 512 * (h + 1)], True, False)
                for k in range(KC):
                    chunk_landed(k)
                    for b in range(2):
                        for h in range(2):
                            last = mm(ps[64 * h:64 * h + 64, b, :], xt[:, k, :],
                                      ring[:, ring_slot(k), b * D + 512 * h:b * D + 512 * (h + 1)], False, k == KC - 1)
                    last.then_inc(chunk_used, 1)
                    if k == 3:
                        pe.wait_ge(y_ready, n + 1)
                        scatter()
                        WT_of[0] = WT[:, wt_slot, :]
                        pe.wait_ge(PW_ready, n + 1)
                        for tt in range(T):
                            last = nc.tensor.transpose(ps[:, 3, tt * P:(tt + 1) * P], PW[:, tt, :], ident[:])
                        last.then_inc(WT_ps, 1)
                gather()
                pe.wait_ge(act_ready, n + 1)
                for f in range(4):
                    last = nc.tensor.transpose(ps[:, 2, f * P:(f + 1) * P], act_out[:, f * P:(f + 1) * P], ident[:])
                last.then_inc(aT_ps, 1)
                pe.wait_ge(aT_ready, n + 1)
                pe.wait_ge(XT_ready, xt_fill)
                for j in range(KC, EXPERT_CHUNKS):
                    chunk_landed(j)
                    for kk in range(2):
                        k = 2 * (j - KC) + kk
                        for hn in range(2):
                            last = mm(ps[64 * hn:64 * hn + 64, 3, :], aT[:, k % 4, BLK * (k // 4):BLK * (k // 4) + BLK],
                                      ring[:, ring_slot(j), kk * D + 512 * hn:kk * D + 512 * (hn + 1)],
                                      k == 0, k == KC - 1)
                    last.then_inc(chunk_used, 1)

            pe.wait_ge(wT_ok, 1)
            pe.wait_ge(late_in, 48)
            pe.wait_ge(P_ready, 1)
            for tt in range(T):
                for hn in range(2):
                    last = mm(ps[:, 4 + 2 * tt + hn, :], wT_sel[:, tt * P:(tt + 1) * P], b_dn[:, 512 * hn:512 * (hn + 1)],
                              True, False, skip_group_check=True)
            last.then_inc(WT_ps, 1)
            for half in range(2):
                if half:
                    pe.wait_ge(XT_ready, 1)
                gather_half(half, 2 * BLK)
            with pe.Fori(0, EXPERTS // 4) as it:
                for q in range(4):
                    n = it * 4 + q

                    def gather():
                        pe.wait_ge(P_ready, it * 2 + (q // 2 + 2))
                        pe.wait_ge(WT_ready, n + 1)
                        gather_half(q % 2, 2 * BLK)

                    if q % 2 == 0:
                        pe.wait_ge(XT_ready, n + 2)
                    expert(n, q % 2, q % 2, (it * 2 + (q // 2 + 1)) * 16,
                           XT[:, q // 2, :, BLK * (q % 2):BLK * (q % 2) + BLK], n + 3, gather)
            n_over = pe.value_load(ovf[0:1, MAX_OVERFLOW:MAX_OVERFLOW + 1], min_val=0, max_val=MAX_OVERFLOW)
            with pe.If(0 < n_over):
                with pe.Fori(0, MAX_OVERFLOW) as b:
                    with pe.If(b < n_over):
                        n = b + EXPERTS
                        pe.wait_ge(P_ready, b + (EXPERTS // 2 + 2))
                        pe.wait_ge(y_ready, n + 1)
                        for half in range(2):
                            pe.wait_ge(XT_ready, b * 2 + (EXPERTS + 2 + half))
                            gather_half(half, BLK)
                        pe.wait_ge(XT_ready, b * 2 + (EXPERTS + 4))
                        WT_of[0] = WT[:, 1, :]
                        expert(n, 1, 0, (b + (EXPERTS // 2 + 1)) * 16, XT[:, 0, :, 0:BLK], b * 2 + (EXPERTS + 4),
                               lambda: pe.wait_ge(WT_ready, n + 1))
            pe.wait_ge(y_ready, EXPERTS + 1)
            with pe.If(0 < n_over):
                pe.wait_ge(y_ready, n_over + (EXPERTS + 1))
            WT_of[0] = WT[:, 1, :]
            scatter()

        @block.scalar
        def _(act):
            def square_sums(src, junk, m):
                for tt in range(T):
                    last = nc.scalar.activation(junk[:, tt, :], src[:, tt, :], ACT.Square, accum_out=sumsq[:, m, tt:tt + 1])
                last.then_inc(sq_done, 1)
                act.wait_ge(sq_done, m + 1)
                nc.scalar.activation(rstd[:, m, :], sumsq[:, m, :], ACT.Sqrt, scale=1.0 / D, bias=eps[:, 0:1]
                                     ).then_inc(std_ready, 1)

            def hT_evac(dst, turn_no, gain):
                for k in (2, 3, 6, 7):
                    act.wait_ge(turned, 4 * turn_no + k // 2 + 1)
                    bank = {0: 0, 1: 4, 2: 4, 3: 2}[turn_no] + k // 2
                    src = ps[:, bank, (k % 2) * S:(k % 2 + 1) * S]
                    if gain is None:
                        i = nc.scalar.copy(dst[:, k, :], src)
                    else:
                        i = nc.scalar.mul(dst[:, k, :], src, g_cols[:, gain * KC + k:gain * KC + k + 1])
                    i.then_inc(hT_act, 1)

            act.wait_ge(eps_ready, 1)
            act.wait_ge(mem_in, 16)
            square_sums(mem_raw, mem_n, 0)
            act.wait_ge(x_in, 16)
            square_sums(x, xn, 1)
            act.wait_ge(gcols_ok, 1)
            hT_evac(mT, 0, 0)
            hT_evac(hT, 1, 1)

            def exps(u):
                kind, j, g = UNITS[u]
                o = OUTPUT_OF[u]
                act.wait_ge(max_ready, o + 1)
                for hh in range(2):
                    for tt in range(T):
                        p = scores[:, u % 4, hh, tt, :]
                        last = nc.scalar.activation(p, p, ACT.Exp, bias=neg_max[:, o, 2 * hh + tt:2 * hh + tt + 1],
                                                    accum_out=exp_sum[:, u, 2 * hh + tt:2 * hh + tt + 1])
                last.then_inc(exp_done, 1)

            for i, (kind, n) in enumerate(FRONT):
                if kind in ("mem", "in"):
                    act.wait_ge(chunk_used, i + 1)
                    if i == 4:
                        act.wait_ge(t5_saved, 16)
                    src = ps[:, i % 2, :].rearrange("p (t c) -> p t c", t=2)
                    if kind == "mem":
                        if n < 2:
                            e = nc.scalar.copy(mkT[:, 2 * n:2 * n + 2, :], src)
                        else:
                            e = nc.scalar.copy(mv[:, :, (n - 2) * 256:(n - 1) * 256], src)
                    elif n in Q_SCALE and n < 15:
                        e = nc.scalar.mul(qkT[:, QKT[n]:QKT[n] + 2, :].rearrange("p b (t q) -> p b t q", t=T),
                                          reversed_tiles(src), Q_SCALE[n])
                    elif n in QKT:
                        e = nc.scalar.mul(qkT[:, QKT[n]:QKT[n] + 2, :], src, Q_SCALE.get(n, 1.0))
                    elif n in V_COL:
                        e = nc.scalar.copy(v[:, :, V_COL[n]:V_COL[n] + 256], src)
                    else:
                        buf, c = GATE_BRANCH[n]
                        e = nc.scalar.activation(gates[:, buf, :, c * 256:(c + 1) * 256], src, ACT.Sigmoid)
                    e.then_inc(front_evac, 1)
                if i in STEP_AFTER:
                    s = STEP_AFTER[i]
                    u = s - TURN_LAG
                    if 0 <= u < NU:
                        act.wait_ge(probs_turned, u + 1)
                        if u >= 2:
                            act.wait_ge(pv_done, u - 1)
                        nc.scalar.copy(pT[:, u % 2, 1], ps[:, 7, :].rearrange("p (k q) -> p k q", k=2)).then_inc(pT_act, 1)
                    if s < NU and s == last_unit_of(OUTPUT_OF[s]):
                        for w in range(NU):
                            if OUTPUT_OF[w] == OUTPUT_OF[s]:
                                exps(w)
                    u = s - PV_LAG
                    if 0 <= u < NU and u == last_unit_of(OUTPUT_OF[u]):
                        kind_u, j, g = UNITS[u]
                        o = OUTPUT_OF[u]
                        act.wait_ge(pv_done, u + 1)
                        if kind_u == "C":
                            e = nc.scalar.copy(qkT[:, 20 + 2 * j:22 + 2 * j, :],
                                               ps[:, 4 + o % 2, :].rearrange("p (h q) -> p h q", h=2))
                        else:
                            e = nc.scalar.copy(qkT[:, j + (8 if kind_u == "B" else 0), :].rearrange("p (t q) -> p t q", t=T),
                                               reversed_tiles(ps[:, 4 + o % 2, 0:S]))
                        e.then_inc(out_evac, 1)
            hT_evac(hT, 2, None)
            act.wait_ge(x1_ready, 1)
            square_sums(x, xn, 2)
            hT_evac(hT, 3, 2)
            act.wait_ge(top_ready, 1)
            for tt in range(T):
                last = nc.scalar.activation(prob[:, tt, :], logits[:, tt, 0:EXPERTS], ACT.Exp, bias=neg_top[:, tt:tt + 1])
            last.then_inc(probs_exp, 1)

            def move_gathered(half, xt, width, count_before):
                act.wait_ge(gathered, count_before + 1)
                for k in range(4):
                    c = 4 * half + k
                    last = nc.scalar.mul(xt[:, c, 0:width], ps[:, 3, k * P:k * P + width],
                                         g_cols[:, 2 * KC + c:2 * KC + c + 1])
                last.then_inc(XT_ready, 1)

            for half in range(2):
                move_gathered(half, XT[:, 0], 2 * BLK, half)

            def expert(n, wt_slot, gathered_next):
                act.wait_ge(WT_ps, n + 2)
                nc.scalar.copy(WT[:, wt_slot, :], ps[:, 3, 0:S]).then_inc(WT_ready, 1)
                act.wait_ge(gate_ready, n + 1)
                nc.scalar.activation(sig, gate_c, ACT.Sigmoid, scale=ALPHA).then_inc(sig_ready, 1)
                gathered_next()
                act.wait_ge(chunk_used, NF + EXPERT_CHUNKS * (n + 1))
                nc.scalar.copy(y_sb, ps[:, 3, :]).then_inc(y_ready, 1)

            with act.Fori(0, EXPERTS // 4) as it:
                for q in range(4):
                    n = it * 4 + q
                    expert(n, q % 2, lambda: move_gathered(q % 2, XT[:, (q // 2 + 1) % 2], 2 * BLK, n + 2))
            n_over = act.value_load(ovf[0:1, MAX_OVERFLOW:MAX_OVERFLOW + 1], min_val=0, max_val=MAX_OVERFLOW)
            with act.If(0 < n_over):
                with act.Fori(0, MAX_OVERFLOW) as b:
                    with act.If(b < n_over):
                        for half in range(2):
                            move_gathered(half, XT[:, 0], BLK, b * 2 + (EXPERTS + 2 + half))
                        expert(b + EXPERTS, 1, lambda: None)
            act.wait_ge(x1_ready, 2)
            square_sums(x, final, 3)

        @block.vector
        def _(dve):
            vec = nc.vector
            links = [0]

            def link(i):
                links[0] += 1
                i.then_inc(dve_chain, 1)
                dve.wait_ge(dve_chain, links[0])

            def normalise(src, dst, m):
                dve.wait_ge(std_ready, m + 1)
                link(vec.reciprocal(rstd[:, m, :], rstd[:, m, :]))
                for tt in range(T):
                    last = vec.tensor_scalar(dst[:, tt, :], src[:, tt, :], rstd[:, m, tt:tt + 1], None, ALU.mult)
                last.then_inc(normed, 1)

            def hT_evac(dst, turn_no, gain):
                for k in (0, 1, 4, 5):
                    dve.wait_ge(turned, 4 * turn_no + k // 2 + 1)
                    bank = {0: 0, 1: 4, 2: 4, 3: 2}[turn_no] + k // 2
                    src = ps[:, bank, (k % 2) * S:(k % 2 + 1) * S]
                    if gain is None:
                        i = vec.tensor_copy(dst[:, k, :], src)
                    else:
                        i = vec.tensor_scalar(dst[:, k, :], src, g_cols[:, gain * KC + k:gain * KC + k + 1], None, ALU.mult)
                    i.then_inc(hT_dve, 1)

            vec.memset(eps[:], EPS).then_inc(eps_ready, 1)
            link(vec.memset(ones[:], 1.0))
            dve.wait_ge(t5_ps, 1)
            vec.tensor_copy(t5_rows, ps[0:DIL_HEADS, 7, :]).then_inc(t5_copied, 1)
            dve.wait_ge(gcols_ps, 1)
            vec.tensor_copy(g_cols[:, 0:3 * KC], ps[:, 6, 0:3 * KC]).then_inc(gcols_ok, 1)
            normalise(mem_raw, mem_n, 0)
            normalise(x, xn, 1)
            dve.wait_ge(gcols_ok, 1)
            hT_evac(mT, 0, 0)
            hT_evac(hT, 1, 1)

            for i, (kind, n) in enumerate(FRONT):
                if kind.startswith("branch"):
                    dve.wait_ge(chunk_used, i + 1)
                    dve.wait_ge(front_evac, i)
                    for half in range(2 if kind == "branch_b" else 1):
                        lo = 512 * (half if kind == "branch_b" else n)
                        y = ps[:, 2 * half:2 * half + 2, :]
                        m = xn[:, :, lo:lo + 512]
                        g = gates[:, 1 if kind == "branch_c" else 0, :, lo:lo + 512]
                        if kind == "branch_a":
                            last = vec.tensor_tensor(m, g, y, ALU.mult)
                        else:
                            link(vec.tensor_tensor(g, g, y, ALU.mult))
                            last = vec.tensor_tensor(m, m, g, ALU.add)
                            if kind == "branch_b":
                                last.then_inc(merged_ready, 1)
                    if kind == "branch_b":
                        dve.wait_ge(merged_ready, 2)
                        last = vec.memset(b_tmp[:], 0.0)
                    last.then_inc(front_evac, 1)
                if kind == "out":
                    dve.wait_ge(chunk_used, i + 1)
                    xs = x[:, :, n * SLOTS_W:(n + 1) * SLOTS_W]
                    vec.tensor_tensor(xs, xs, ps[:, i % 2, :].rearrange("p (t c) -> p t c", t=2), ALU.add
                                      ).then_inc(front_evac, 1)
                if i in STEP_AFTER:
                    s = STEP_AFTER[i]
                    if s < NU:
                        kind_u, j, g = UNITS[s]
                        dve.wait_ge(scores_ready, s + 1)
                        if s >= 4:
                            dve.wait_ge(probs_turned, s - 3)
                        if kind_u != "C":
                            b = (s - 2) % 4
                            dve.wait_ge(image_in[b], 16 * ((s - 2) // 4 + 1))
                            if kind_u == "A":
                                im = image[:, b].rearrange("p h (r c) -> p (h r) c", c=GRID_W)
                                link(vec.tensor_tensor(im, im, bcast(na_mask[:], 1, 2 * IMG // GRID_W), ALU.add))
                        for tt in range(T):
                            src = ps[:, 2:4, tt * S:(tt + 1) * S]
                            dst = scores[:, s % 4, :, tt, :]
                            if kind_u == "C":
                                last = vec.tensor_copy(dst, src)
                            else:
                                last = vec.tensor_tensor(dst, src, image[:, b, :, P - P * tt:P - P * tt + S], ALU.add)
                        last.then_inc(scores_drained, 1)
                        dve.wait_ge(scores_drained, s + 1)
                        link(vec.tensor_reduce(row_max[:, s, :], scores[:, s % 4].rearrange("p h t k -> p (h t) k"),
                                               AX_X, ALU.max))
                        o = OUTPUT_OF[s]
                        if s == last_unit_of(o):
                            if kind_u == "B":
                                link(vec.tensor_tensor(b_tmp[:, 0, :], row_max[:, s - 2, :], row_max[:, s - 1, :], ALU.max))
                                link(vec.tensor_tensor(row_max[:, s, :], b_tmp[:, 0, :], row_max[:, s, :], ALU.max))
                            vec.tensor_scalar(neg_max[:, o, :], row_max[:, s, :], -1.0, None, ALU.mult).then_inc(max_ready, 1)
                    u = s - TURN_LAG
                    if 0 <= u < NU:
                        dve.wait_ge(probs_turned, u + 1)
                        if u >= 2:
                            dve.wait_ge(pv_done, u - 1)
                        vec.tensor_copy(pT[:, u % 2, 0], ps[:, 6, :].rearrange("p (k q) -> p k q", k=2)).then_inc(pT_dve, 1)
                    if s < NU and s == last_unit_of(OUTPUT_OF[s]):
                        o = OUTPUT_OF[s]
                        dve.wait_ge(exp_done, s + 1)
                        total = exp_sum[:, s, :]
                        if UNITS[s][0] == "B":
                            link(vec.tensor_tensor(b_tmp[:, 0, :], exp_sum[:, s - 2, :], exp_sum[:, s - 1, :], ALU.add))
                            link(vec.tensor_tensor(b_tmp[:, 1, :], b_tmp[:, 0, :], exp_sum[:, s, :], ALU.add))
                            total = b_tmp[:, 1, :]
                        link(vec.reciprocal(inv_sum[:, o, :], total))
                        for w in range(NU):
                            if OUTPUT_OF[w] == o:
                                p = scores[:, w % 4].rearrange("p h t k -> p (h t) k")
                                vec.tensor_tensor(p, p, bcast(inv_sum[:, o, :], 2, S), ALU.mult).then_inc(probs_ready, 1)
                if kind == "branch_b":
                    hT_evac(hT, 2, None)
            dve.wait_ge(front_evac, NF)
            vec.memset(eps[:], EPS).then_inc(x1_ready, 1)
            normalise(x, xn, 2)
            hT_evac(hT, 3, 2)

            link(vec.memset(logits[:, :, EXPERTS:], SENTINEL))
            link(vec.memset(keys[:, :, EXPERTS:], -NO_SLOT))
            vec.memset(WT[:, 1, :], 0.0)
            vec.memset(y_sb, 0.0).then_inc(y_ready, 1)
            vec.memset(b_tmp[:], 0.0).then_inc(gu_drained, 1)
            dve.wait_ge(router_ps, 1)
            dve.wait_ge(late_in, 48)
            link(vec.tensor_tensor(logits[:, :, 0:EXPERTS], ps[:, 6, 0:T * EXPERTS].rearrange("p (t e) -> p t e", t=T),
                                   bcast(rb[:], 1, T), ALU.add))
            for tt in range(T):
                link(vec.max(top8[:, tt, :], logits[:, tt, :]))
            vec.tensor_scalar(neg_top, top8[:, :, 0], -1.0, None, ALU.mult).then_inc(top_ready, 1)
            link(vec.memset(top8[:, :, TOP_K:], SENTINEL))
            for tt in range(T):
                link(vec.match_replace(replaced[:, tt, :], top8[:, tt, :], logits[:, tt, :], REPLACED))
            vec.tensor_tensor(mask, replaced[:, :, 0:EXPERTS], logits[:, :, 0:EXPERTS], ALU.not_equal).then_inc(mask_ready, 1)
            dve.wait_ge(mask_ready, 1)
            dve.wait_ge(probs_exp, 1)
            link(vec.tensor_tensor(prob_m, prob, mask, ALU.mult))
            link(vec.tensor_reduce(w_sum, prob_m, AX_X, ALU.add))
            link(vec.reciprocal(w_inv, w_sum))
            vec.tensor_tensor(w_sel, prob_m, bcast(w_inv, 2, EXPERTS), ALU.mult).then_inc(wsel_ready, 1)
            dve.wait_ge(rank_ps, 1)
            link(vec.tensor_scalar(tmp_a, mask, NO_SLOT, -NO_SLOT, ALU.mult, ALU.add))
            link(vec.tensor_tensor(keys[:, :, 0:EXPERTS], tmp_a, ps[:, 7, 0:T * EXPERTS].rearrange("p (t e) -> p t e", t=T),
                                   ALU.add))
            link(vec.tensor_copy(count, ps[:, 7, 64:64 + EXPERTS]))

            def gather_matrix(col, width, slots):
                for tt in range(T):
                    last = vec.tensor_scalar(P_pair[:, tt, col:col + width], slots, keys_at[0][:, tt, keys_at[1]], None,
                                             ALU.is_equal)
                return last

            keys_at = [keys, slice(0, 1)]
            gather_matrix(0, BLK, iota[:, 0:BLK])
            keys_at[1] = slice(1, 2)
            gather_matrix(BLK, BLK, iota[:, 0:BLK]).then_inc(P_ready, 1)
            dve.wait_ge(wT_ps, 1)
            vec.tensor_copy(wT_sel, ps[0:EXPERTS, 1, 0:S]).then_inc(wT_ok, 1)
            link(vec.tensor_scalar(extra, count, float(BLK), None, ALU.is_gt))
            for lim in (2 * BLK, 3 * BLK):
                link(vec.tensor_scalar(tmp_a[:, 0, :], count, float(lim), None, ALU.is_gt))
                link(vec.tensor_tensor(extra, extra, tmp_a[:, 0, :], ALU.add))
            link(vec.tensor_tensor_scan(ends, extra, extra, 0.0, ALU.add, ALU.bypass))
            link(vec.tensor_tensor(tmp_a[:, 0, :], ends, extra, ALU.subtract))
            link(vec.tensor_scalar(tmp_a[:, 0, :], tmp_a[:, 0, :], float(BLK), NO_SLOT - BLK, ALU.mult, ALU.add))
            link(vec.tensor_tensor(okeys, keys[:, :, 0:EXPERTS], bcast(tmp_a[:, 0, :], 1, T), ALU.add))
            link(vec.tensor_scalar(tmp_b, keys[:, :, 0:EXPERTS], float(BLK), None, ALU.is_ge))
            link(vec.tensor_tensor(okeys, okeys, tmp_b, ALU.mult))
            link(vec.tensor_scalar(okeys, okeys, NO_SLOT, None, ALU.subtract))
            link(vec.tensor_tensor(ends_le, bcast(ends, 1, MAX_OVERFLOW), bcast(iota[:, 0:MAX_OVERFLOW], 2, EXPERTS), ALU.is_le))
            link(vec.tensor_reduce(ovf_f, ends_le, AX_X, ALU.add))
            link(vec.tensor_scalar(ovf_f, ovf_f, float(EXPERTS - 1), None, ALU.min))
            link(vec.tensor_copy(ovf[:, 0:MAX_OVERFLOW], ovf_f))
            vec.tensor_copy(ovf[:, MAX_OVERFLOW:], ends[:, EXPERTS - 1:EXPERTS]).then_inc(routed, 1)

            def expert(n, key_tile, slots, e):
                dve.wait_ge(WT_ps, n + 1)
                for tt in range(T):
                    last = vec.tensor_scalar(PW[:, tt, :].rearrange("p (a s) -> p a s", a=2), bcast(slots, 1, 2),
                                             key_tile[:, tt, e], w_sel[:, tt, e], ALU.is_equal, ALU.mult)
                last.then_inc(PW_ready, 1)
                dve.wait_ge(chunk_used, NF + EXPERT_CHUNKS * n + KC)
                vec.tensor_scalar(gate_c, ps[:, 0, :], LIMIT, None, ALU.min).then_inc(gate_ready, 1)
                vec.tensor_scalar(up_c, ps[:, 1, :], -LIMIT, LIMIT, ALU.max, ALU.min).then_inc(gu_drained, 1)
                dve.wait_ge(gate_ready, n + 1)
                dve.wait_ge(gu_drained, n + 2)
                vec.scalar_tensor_tensor(gu_prod, up_c, 1.0, gate_c, ALU.add, ALU.mult).then_inc(prod_ready, 1)
                dve.wait_ge(prod_ready, n + 1)
                dve.wait_ge(sig_ready, n + 1)
                vec.tensor_tensor(act_out, gu_prod, sig, ALU.mult).then_inc(act_ready, 1)
                dve.wait_ge(aT_ps, n + 1)
                vec.tensor_copy(aT, ps[:, 2, :].rearrange("p (f s) -> p f s", f=4)).then_inc(aT_ready, 1)

            with dve.Fori(0, EXPERTS // 4) as it:
                for q in range(4):
                    n = it * 4 + q
                    if q % 2 == 0:
                        dve.wait_ge(gathered, n + 2)
                        for a in range(2):
                            keys_at[1] = bass.ds(n + (2 + a), 1)
                            last = gather_matrix(BLK * a, BLK, iota[:, 0:BLK])
                        last.then_inc(P_ready, 1)
                    expert(n, keys, iota[:, 0:BLK], bass.ds(n, 1))
            dve.wait_ge(routed, 1)
            n_over = dve.value_load(ovf[0:1, MAX_OVERFLOW:MAX_OVERFLOW + 1], min_val=0, max_val=MAX_OVERFLOW)
            with dve.If(0 < n_over):
                with dve.Fori(0, MAX_OVERFLOW) as b:
                    with dve.If(b < n_over):
                        e_b = dve.value_load(ovf[0:1, bass.ds(b, 1)], min_val=0, max_val=EXPERTS - 1)
                        slots = iota[:, bass.ds(b * BLK, BLK)]
                        dve.wait_ge(gathered, b * 2 + (EXPERTS + 2))
                        keys_at[0], keys_at[1] = okeys, bass.ds(e_b, 1)
                        gather_matrix(0, BLK, slots).then_inc(P_ready, 1)
                        expert(b + EXPERTS, okeys, slots, bass.ds(e_b, 1))
            dve.wait_ge(scattered, EXPERTS + 1)
            with dve.If(0 < n_over):
                dve.wait_ge(scattered, n_over + (EXPERTS + 1))
                vec.memset(b_tmp[:], 0.0)
            y = ps[:, 4:8, :].rearrange("p (t h) c -> p t (h c)", t=T)
            vec.tensor_tensor(x[:], x[:], y, ALU.add).then_inc(x1_ready, 1)
            dve.wait_ge(x1_ready, 2)
            dve.wait_ge(std_ready, 4)
            link(vec.reciprocal(rstd[:, 3, :], rstd[:, 3, :]))
            for tt in range(T):
                last = vec.scalar_tensor_tensor(final[:, tt, :], x[:, tt, :], rstd[:, 3, tt:tt + 1], final_g,
                                                ALU.mult, ALU.mult)
            last.then_inc(final_ready, 1)


def t5_bucket(rel):
    half = T5_BUCKETS // 2
    exact = half // 2
    n = np.abs(rel)
    large = exact + (np.log(np.maximum(n, 1).astype(np.float32) / exact) / math.log(T5_MAX_DIST / exact)
                     * (half - exact)).astype(np.int32)
    return np.where(rel > 0, half, 0) + np.where(n < exact, n, np.minimum(large, half - 1))


def constants():
    rel = np.arange(REL) - (S - 1)
    onehot = np.zeros((T5_BUCKETS + 3, REL), np.float32)
    onehot[t5_bucket(rel), np.arange(REL)] = 1.0
    for g, (dil, window) in enumerate(zip(DIL, DIL_WINDOW)):
        ok = (rel % dil == 0) & (np.abs(rel) // dil <= window // 2 // dil)
        onehot[T5_BUCKETS + g] = np.where(ok, 0.0, NEG)
    group = np.zeros((3, DIL_HEADS), np.float32)
    for g in range(3):
        group[g, g * GROUP_HEADS:(g + 1) * GROUP_HEADS] = 1.0
    col = np.arange(GRID_W)
    start = np.clip(col - WIN_COLS // 2, 0, GRID_W - WIN_COLS)
    ok = (col[None] >= start[:, None]) & (col[None] < start[:, None] + WIN_COLS)
    na_mask = np.tile(np.where(ok, 0.0, NEG).astype(np.float32), (P // GRID_W, 1))[::-1].copy()
    return {"bucket_onehot": onehot, "group_of_head": group, "na_mask": na_mask, "ident": np.eye(P, dtype=np.float32),
            "earlier": np.triu(np.ones((P, P), np.float32), 1), "iota": np.arange(D, dtype=np.float32)}


_DIRECT = ["x", "mem", "w_in", "w_mem_kv", "t5_rel_bias", "w_branch_a", "w_branch_b", "w_branch_c", "w_out", "router_w",
           "router_b", "expert_w_gate_up", "expert_b_gate_up", "expert_w_down", "expert_b_down", "final_norm_g"]


def kernel(**inputs):
    import concourse.bacc as bacc
    from concourse.bass_utils import run_bass_kernel_spmd

    arrays = {n: np.ascontiguousarray(inputs[n]) for n in _DIRECT}
    arrays.update(constants())
    arrays["g_rows"] = np.concatenate([np.asarray(inputs[n]).reshape(KC, P)
                                       for n in ("mem_norm_g", "attn_norm_g", "ffn_norm_g")], 0)
    rpb = np.asarray(inputs["na_rpb"])[0]
    rows = np.zeros((NA_HEADS, REL), rpb.dtype)
    dc = np.arange(-(WIN_COLS - 1), WIN_COLS)
    for dr in range(-(S // GRID_W - 1), S // GRID_W):
        rows[:, GRID_W * dr + dc + S - 1] = rpb[:, dr + WIN_ROWS - 1, :]
    arrays["na_rows"] = rows
    nc = bacc.Bacc("TRN2", target_bir_lowering=False, num_devices=1)
    t = {n: nc.dram_tensor(f"in_{n}", a.shape, mybir.dt.from_np(a.dtype), kind="ExternalInput").ap()
         for n, a in arrays.items()}
    t["out"] = nc.dram_tensor("out_0", (1, S, D), F32, kind="ExternalOutput").ap()
    build(nc, t)
    r = run_bass_kernel_spmd(nc, [{f"in_{n}": a for n, a in arrays.items()}], core_ids=[0])
    return np.asarray(r.results[0]["out_0"])
```

```python
import math
from contextlib import ExitStack

import numpy as np
import concourse.bass as bass
from concourse import mybir

F32 = mybir.dt.float32
I32 = mybir.dt.int32
ALU = mybir.AluOpType
ACT = mybir.ActivationFunctionType
AX_X = mybir.AxisListType.X

P = 128
D = 1024
KC = D // P
S = 256
T = S // P
MEM = 256
GRID_W, WIN_COLS, WIN_ROWS = 64, 16, 8
NA_HEADS, HD = 8, 64
DIL = (1, 4, 16)
DIL_WINDOW = (128, 512, 2048)
GROUP_HEADS = 4
DIL_HEADS = GROUP_HEADS * len(DIL)
MEM_HEADS, MEM_HD = 4, 128
T5_BUCKETS, T5_MAX_DIST = 32, 1024
EXPERTS, TOP_K = 32, 4
ALPHA, LIMIT, EPS = 1.702, 7.0, 1e-6
NEG = -1e30
SENTINEL = -3e38
REPLACED = -3.2e38
NO_SLOT = 4096.0

BLK = 64
CHUNK = 2048
RING = 16
FRONT_RING = 10
SCORE_SLOTS = 2
EXPERT_CHUNKS = 12
MAX_OVERFLOW = S * TOP_K // BLK
REL = 2 * S
IMG = 3 * P
SLOTS_W = 256

FRONT = ([("mem", i) for i in range(4)] + [("in", i) for i in (15, 16)] + [("in", i) for i in range(15)]
         + [("in", i) for i in range(17, 21)] + [("branch_a", 0), ("branch_a", 1)]
         + [("in", i) for i in range(25, 29)] + [("branch_c", 0), ("branch_c", 1)]
         + [("in", i) for i in range(21, 25)] + [("branch_b", 0)] + [("out", i) for i in range(4)])
NF = len(FRONT)
OUT0 = NF - 4
UNITS = [("C", 0, 0), ("C", 1, 0)] + [("A", j, 0) for j in range(4)] + [("B", j, g) for j in range(2) for g in range(3)]
NU = len(UNITS)
OUTPUT_OF = [0, 1, 2, 3, 4, 5, 6, 6, 6, 7, 7, 7]
TURN_LAG, PV_LAG = 3, 4
STEP_AFTER = {6: 0, 7: 1, 11: 2, 12: 3, 13: 4, 14: 5, 20: 6, 21: 7, 22: 8, 23: 9, 24: 10, 27: 11, 28: 12, 29: 13,
              30: 14, 31: 15}
QKT = {0: 0, 1: 2, 2: 4, 3: 6, 6: 8, 7: 10, 8: 12, 9: 14, 10: 16, 11: 18, 15: 20, 16: 22}
V_COL = {4: 0, 5: 256, 12: 512, 13: 768, 14: 1024}
Q_SCALE = {0: HD ** -0.5, 1: HD ** -0.5, 6: HD ** -0.5, 7: HD ** -0.5, 8: HD ** -0.5,
           15: MEM_HD ** -0.5, 16: MEM_HD ** -0.5}
GATE_BRANCH = {**{i: (0, i - 17) for i in range(17, 21)}, **{i: (1, i - 25) for i in range(25, 29)},
               **{i: (0, i - 21) for i in range(21, 25)}}


def image_rows(u):
    kind, j, g = UNITS[u]
    return 2 * j if kind == "A" else NA_HEADS + g * GROUP_HEADS + 2 * j


def unit_blocks(u):
    kind, j, g = UNITS[u]
    if kind == "A":
        return j, 4 + j, 128 * j
    b = g * 2 + j
    return 8 + b, 14 + b, 512 + 128 * b


def last_unit_of(o):
    return max(u for u in range(NU) if OUTPUT_OF[u] == o)


def build(nc, t):
    w_in = t["w_in"].rearrange("l (k p) c -> (l p) k c", p=P)
    w_mem = t["w_mem_kv"].rearrange("l (k p) c -> (l p) k c", p=P)
    w_out = t["w_out"].rearrange("l (k p) c -> (l p) k c", p=P)
    w_br = {b: t[f"w_{b}"].rearrange("l (k p) c -> (l p) k c", p=P) for b in ("branch_a", "branch_b", "branch_c")}
    w_gu = t["expert_w_gate_up"].rearrange("l e (k p) c -> (l e) p k c", p=P)
    w_dn = t["expert_w_down"].rearrange("l e (k p) c -> (l e) p k c", p=P)
    b_gu = t["expert_b_gate_up"]
    na_rows = t["na_rows"]
    t5_scratch = nc.dram_tensor("t5_scratch", [DIL_HEADS, REL], F32, kind="Internal").ap()

    with ExitStack() as ctx:
        def sb(name, shape, dt=F32):
            return ctx.enter_context(nc.sbuf_tensor(name, shape, dt))

        def sem(name):
            return ctx.enter_context(nc.semaphore(name))

        FRONT0, MOE0 = (FRONT_RING + SCORE_SLOTS) * CHUNK, RING * CHUNK
        arena = sb("arena", [P, FRONT0 + 20480])
        ring = arena[:, 0:RING * CHUNK].rearrange("p (r c) -> p r c", r=RING)
        ident = sb("ident", [P, P])
        earlier = sb("earlier", [P, P])
        ones = sb("ones", [P, P])
        na_mask = sb("na_mask", [P, GRID_W])
        g_rows = sb("g_rows", [3 * KC, P])
        g_cols = sb("g_cols", [P, 4 * KC])
        eps = sb("eps", [P, 1])
        x = sb("x_tokens", [P, T, D])
        xn = sb("x_normed", [P, T, D])
        hT = sb("h_T", [P, KC, S])
        rw = sb("router_w_sb", [P, KC, EXPERTS])
        rb = sb("router_b_sb", [P, EXPERTS])
        stack4 = sb("stack4", [P, EXPERTS])
        sumsq = sb("sumsq", [P, 4, T])
        rstd = sb("rstd", [P, 4, T])
        onehot = sb("onehot", [T5_BUCKETS + 3, REL])
        t5_in = sb("t5_in", [T5_BUCKETS + 3, DIL_HEADS])
        row_max = sb("row_max", [P, NU, 4])
        neg_max = sb("neg_max", [P, 8, 4])
        exp_sum = sb("exp_sum", [P, NU, 4])
        inv_sum = sb("inv_sum", [P, 8, 4])
        b_tmp = sb("b_tmp", [P, 2, 4])

        def area(off, *dims):
            n = int(np.prod(dims))
            assert off + n <= FRONT0 + 20480
            flat = arena[:, off:off + n]
            if len(dims) == 2:
                return flat.rearrange("p (a b) -> p a b", a=dims[0])
            if len(dims) == 3:
                return flat.rearrange("p (a b c) -> p a b c", a=dims[0], b=dims[1])
            if len(dims) == 4:
                return flat.rearrange("p (a b c d) -> p a b c d", a=dims[0], b=dims[1], c=dims[2])
            return flat

        image = area(FRONT0, 4, 2, IMG)
        pT = area(FRONT0 + 3072, 2, 2, 2, S)
        qkT = area(FRONT0 + 5120, 24, S)
        v = area(FRONT0 + 11264, T, 1280)
        mkT = area(FRONT0 + 13824, MEM_HEADS, MEM)
        mv = area(FRONT0 + 14848, T, MEM_HEADS * MEM_HD)
        gates = area(FRONT0 + 15872, 2, T, D)
        mem_raw = area(FRONT0 + 3072, T, D)
        mem_n = area(FRONT0 + 15872, T, D)
        t5_rows = area(FRONT0 + 15872, REL)[0:DIL_HEADS, :]
        mT = area(FRONT0 + 15872 + 2048, KC, MEM)
        scores = ring[:, FRONT_RING:FRONT_RING + SCORE_SLOTS, :].rearrange("p a (b h t k) -> p (a b) h t k", b=2, h=2, t=2)
        XT = hT[:].rearrange("p k s -> p (k s)").rearrange("p (b k s) -> p b k s", b=2, k=KC)
        place = [MOE0]

        def moe(*dims):
            at = place[0]
            place[0] += int(np.prod(dims))
            return area(at, *dims)

        brow = moe(2 * D)
        b_dn = moe(D)[0:EXPERTS, :]
        final_g = moe(D)
        iota = moe(D)
        x1T = area(place[0], KC, S)
        P_pair = moe(T, 2 * BLK)
        PW = moe(T, 2 * BLK)
        WT = moe(2, S)
        gate_c, up_c, sig = moe(512), moe(512), moe(512)
        aT = moe(4, P)
        y_sb = moe(512)
        logits, top8, replaced = moe(T, 40), moe(T, 8), moe(T, 40)
        mask, neg_top = moe(T, EXPERTS), moe(T)
        prob, prob_m, w_sum, w_inv, w_sel = moe(T, EXPERTS), moe(T, EXPERTS), moe(T), moe(T), moe(T, EXPERTS)
        keys = moe(T, EXPERTS + 4)
        okeys = moe(T, EXPERTS)
        count, extra, ends = moe(EXPERTS), moe(EXPERTS), moe(EXPERTS)
        tmp_a, tmp_b = moe(T, EXPERTS), moe(T, EXPERTS)
        ends_le = moe(MAX_OVERFLOW, EXPERTS)
        ovf_f = moe(MAX_OVERFLOW)
        wT_sel = moe(S)[0:EXPERTS, :]
        router_parts = moe(S)
        sq_tmp = moe(T, SLOTS_W)
        part_sums = moe(T, 4)
        final = xn[:]
        ovf = sb("ovf", [P, MAX_OVERFLOW + 1], I32)

        ps = ctx.enter_context(nc.psum_tensor("ps", [P, 8, 512], F32))

        landed = [sem(f"landed{i}") for i in range(RING)]
        first_in, t5_in_done, consts_in = sem("first_in"), sem("t5_in_done"), sem("consts_in")
        mem_in = sem("mem_in")
        x_in = sem("x_in")
        t5_saved = sem("t5_saved")
        image_in = [sem(f"image_in{i}") for i in range(4)]
        late_in = sem("late_in")
        brow_in = [sem(f"brow_in{i}") for i in range(2)]
        out_saved = sem("out_saved")
        chunk_used = sem("chunk_used")
        gcols_ps, gcols_ok = sem("gcols_ps"), sem("gcols_ok")
        t5_ps, t5_copied = sem("t5_ps"), sem("t5_copied")
        rstd_ready, x1T_act, x1T_dve, parts_ps, parts_in, square_parts = (
            sem("rstd_ready"), sem("x1T_act"), sem("x1T_dve"), sem("parts_ps"), sem("parts_in"), sem("square_parts"))
        x1_turned = sem("x1_turned")
        normed = sem("normed")
        turned = sem("turned")
        hT_act, hT_dve = sem("hT_act"), sem("hT_dve")
        sums_ready = sem("sums_ready")
        sq_done, std_ready = sem("sq_done"), sem("std_ready")
        probs_exp = sem("probs_exp")
        front_evac = sem("front_evac")
        scores_ready, scores_drained = sem("scores_ready"), sem("scores_drained")
        max_ready, exp_done, probs_ready = sem("max_ready"), sem("exp_done"), sem("probs_ready")
        probs_turned, pT_dve, pT_act = sem("probs_turned"), sem("pT_dve"), sem("pT_act")
        pv_done, out_evac = sem("pv_done"), sem("out_evac")
        merged_ready = sem("merged_ready")
        x1_ready = sem("x1_ready")
        router_ps, top_ready = sem("router_ps"), sem("top_ready")
        mask_ready, rank_ps, wsel_ready = sem("mask_ready"), sem("rank_ps"), sem("wsel_ready")
        wT_ps, wT_ok = sem("wT_ps"), sem("wT_ok")
        routed = sem("routed")
        P_ready, gathered, XT_ready = sem("P_ready"), sem("gathered"), sem("XT_ready")
        PW_ready, WT_ps, WT_ready = sem("PW_ready"), sem("WT_ps"), sem("WT_ready")
        gate_ready, gu_drained, sig_ready = sem("gate_ready"), sem("gu_drained"), sem("sig_ready")
        prod_ready, act_ready = sem("prod_ready"), sem("act_ready")
        aT_ps, aT_ready, y_ready, scattered = sem("aT_ps"), sem("aT_ready"), sem("y_ready"), sem("scattered")
        final_ready = sem("final_ready")
        dve_chain = sem("dve_chain")
        eps_ready = sem("eps_ready")

        block = ctx.enter_context(nc.Block())

        def front_landed(eng, i):
            eng.wait_ge(landed[i % FRONT_RING], 16 * (i // FRONT_RING + 1))

        def ring_slot(c):
            return (c + NF % FRONT_RING) % RING

        def front_fills(r):
            return len(range(r, NF, FRONT_RING)) if r < FRONT_RING else 0


        def bcast(ap, axis, n):
            dims = [list(d) for d in ap.ap]
            return bass.AP(ap.tensor, ap.offset, dims[:axis] + [[0, n]] + dims[axis:])

        def reversed_tiles(ap):
            dims = [list(d) for d in ap.ap]
            step, n = dims[-1]
            return bass.AP(ap.tensor, ap.offset + (P - 1) * step, dims[:-1] + [[P * step, n // P], [-step, P]])

        @block.sync
        def _(sp):
            sp.dma_start(mem_raw, t["mem"].rearrange("b (t p) d -> (b p) t d", p=P)).then_inc(mem_in, 16)
            sp.dma_start(ident[:], t["ident"]).then_inc(first_in, 16)
            sp.dma_start(g_rows[:], t["g_rows"]).then_inc(first_in, 16)
            for i in range(NF):
                if i == 1:
                    sp.dma_start(x[:], t["x"].rearrange("b (t p) d -> (b p) t d", p=P)).then_inc(x_in, 16)
                    sp.dma_start(t5_in[0:T5_BUCKETS, :], t["t5_rel_bias"]).then_inc(t5_in_done, 16)
                    sp.dma_start(t5_in[T5_BUCKETS:T5_BUCKETS + 3, :], t["group_of_head"]).then_inc(t5_in_done, 16)
                    sp.dma_start(onehot[:], t["bucket_onehot"]).then_inc(t5_in_done, 16)
                if i >= FRONT_RING:
                    sp.wait_ge(chunk_used, i - FRONT_RING + 1)
                kind, n = FRONT[i]
                dst = ring[:, i % FRONT_RING, :]
                if kind in ("mem", "in", "out"):
                    src = {"mem": w_mem, "in": w_in, "out": w_out}[kind][:, :, n * SLOTS_W:(n + 1) * SLOTS_W]
                    dst = dst.rearrange("p (k c) -> p k c", k=KC)
                elif kind == "branch_b":
                    src, dst = w_br[kind], dst.rearrange("p (k c) -> p k c", k=2)
                else:
                    src, dst = w_br[kind][:, :, n * 512:(n + 1) * 512], dst.rearrange("p (k c) -> p k c", k=4)
                sp.dma_start(dst, src).then_inc(landed[i % FRONT_RING], 16)

            def load_expert(e, n, c, bias_slot, wait_for, bias_before=0):
                for j in range(EXPERT_CHUNKS):
                    r = ring_slot(c + j)
                    wait_for(j)
                    if j == bias_before:
                        sp.dma_start(brow[64 * bias_slot:64 * bias_slot + 1, :], b_gu[0, bass.ds(e, 1), :]
                                     ).then_inc(brow_in[bias_slot], 16)
                    if j < KC:
                        src = w_gu[bass.ds(e, 1), :, j, :].rearrange("o p c -> (o p) c")
                        dst = ring[:, r, :]
                    else:
                        src = w_dn[bass.ds(e, 1), :, 2 * (j - KC):2 * (j - KC) + 2, :].rearrange("o p k c -> (o p) k c")
                        dst = ring[:, r, :].rearrange("p (k c) -> p k c", k=2)
                    sp.dma_start(dst, src).then_inc(landed[r], 16)

            def first_lap(n):
                def wait_for(j):
                    c = EXPERT_CHUNKS * n + j
                    r = ring_slot(c)
                    if j == 0 and n >= 2:
                        sp.wait_ge(chunk_used, NF + EXPERT_CHUNKS * (n - 2) + 1)
                    if c == FRONT_RING - 2:
                        sp.wait_ge(pv_done, NU)
                        sp.wait_ge(merged_ready, 2)
                        sp.wait_ge(chunk_used, OUT0)
                    if c >= RING:
                        sp.wait_ge(chunk_used, NF + c - RING + 1)
                    elif r < FRONT_RING:
                        sp.wait_ge(chunk_used, max(i for i in range(NF) if i % FRONT_RING == r) + 1)
                return wait_for

            for e in range(4):
                load_expert(e, e, EXPERT_CHUNKS * e, e % 2, first_lap(e), 0 if e else FRONT_RING - 2)
            with sp.Fori(1, EXPERTS // 4) as it:
                for q in range(4):
                    def wait_for(j):
                        sp.wait_ge(chunk_used, it * (4 * EXPERT_CHUNKS) + (NF + EXPERT_CHUNKS * q + j - RING + 1))
                    load_expert(it * 4 + q, it * 4 + q, EXPERT_CHUNKS * q, q % 2, wait_for)
            sp.wait_ge(routed, 1)
            n_over = sp.value_load(ovf[0:1, MAX_OVERFLOW:MAX_OVERFLOW + 1], min_val=0, max_val=MAX_OVERFLOW)
            with sp.If(0 < n_over):
                with sp.Fori(0, MAX_OVERFLOW) as b:
                    with sp.If(b < n_over):
                        e_b = sp.value_load(ovf[0:1, bass.ds(b, 1)], min_val=0, max_val=EXPERTS - 1)

                        def wait_for(j):
                            sp.wait_ge(chunk_used, b * EXPERT_CHUNKS + (NF + EXPERT_CHUNKS * (EXPERTS - 1) + j + 1))
                        load_expert(e_b, b + EXPERTS, 0, 0, wait_for)
            sp.wait_ge(final_ready, 1)
            sp.dma_start(t["out"].rearrange("b (t p) d -> (b p) t d", p=P), final).then_inc(out_saved, 16)
            sp.wait_ge(out_saved, 16)

        @block.gpsimd
        def _(pool):
            pool.wait_ge(mem_in, 16)
            pool.dma_start(na_mask[:], t["na_mask"]).then_inc(consts_in, 16)
            pool.wait_ge(t5_copied, 1)
            pool.dma_start(t5_scratch, t5_rows).then_inc(t5_saved, 16)
            pool.wait_ge(t5_saved, 16)
            for u in range(2, NU):
                i = u - 2
                if i >= 4:
                    pool.wait_ge(scores_drained, u - 3)
                row = image_rows(u)
                rows, row = (na_rows, row) if row < NA_HEADS else (t5_scratch, row - NA_HEADS)
                pool.dma_start(image[:, i % 4], bass.AP(rows.tensor, row * REL, [[1, P], [REL, 2], [1, IMG]])
                               ).then_inc(image_in[i % 4], 16)
            pool.dma_start(earlier[:], t["earlier"]).then_inc(consts_in, 16)
            pool.dma_start(stack4[:], t["stack4"]).then_inc(consts_in, 16)
            pool.dma_start(rw[:], t["router_w"].rearrange("l (k p) e -> (l p) k e", p=P)).then_inc(consts_in, 16)
            pool.dma_start(rb[:], bass.AP(t["router_b"].tensor, 0, [[0, P], [1, EXPERTS]])).then_inc(consts_in, 16)
            pool.wait_ge(merged_ready, 2)
            pool.wait_ge(chunk_used, OUT0)
            pool.dma_start(b_dn, t["expert_b_down"].rearrange("l e c -> (l e) c")).then_inc(late_in, 16)
            pool.dma_start(final_g, bass.AP(t["final_norm_g"].tensor, 0, [[0, P], [1, D]])).then_inc(late_in, 16)
            pool.dma_start(iota, bass.AP(t["iota"].tensor, 0, [[0, P], [1, D]])).then_inc(late_in, 16)
            pool.wait_ge(rstd_ready, 1)
            for tt in range(T):
                last = nc.gpsimd.tensor_scalar(xn[:, tt, :], x[:, tt, :], rstd[:, 2, tt:tt + 1], None, ALU.mult)
            last.then_inc(normed, 1)

        @block.tensor
        def _(pe):
            def mm(out, lhsT, rhs, start, stop, **kw):
                return nc.tensor.matmul(out, lhsT, rhs, start=start, stop=stop, **kw)

            def turn(src, m, first_bank):
                pe.wait_ge(normed, m + 1)
                for k in range(KC):
                    for tt in range(T):
                        last = nc.tensor.transpose(ps[:, first_bank + k // 2, (k % 2) * S + tt * P:(k % 2) * S + (tt + 1) * P],
                                                   src[:, tt, k * P:(k + 1) * P], ident[:])
                    if k % 2:
                        last.then_inc(turned, 1)

            pe.wait_ge(first_in, 32)
            nc.tensor.transpose(ps[:, 6, 0:3 * KC], g_rows[:], ident[0:3 * KC, 0:3 * KC]).then_inc(gcols_ps, 1)
            turn(mem_n, 0, 0)

            def head_scores(u):
                kind, j, g = UNITS[u]
                pe.wait_ge(front_evac, {"C": 6, "A": 12, "B": 21}[kind])
                if u:
                    pe.wait_ge(scores_drained, u)
                else:
                    pe.wait_ge(hT_act, 8)
                    pe.wait_ge(hT_dve, 8)
                for tt in range(T):
                    for hh in range(2):
                        out = ps[:, 2 + hh, tt * S:(tt + 1) * S]
                        if kind == "C":
                            h = 2 * j + hh
                            last = mm(out, qkT[:, 20 + h, tt * P:(tt + 1) * P], mkT[:, h, :], True, True)
                        else:
                            qb, kb, _ = unit_blocks(u)
                            rows = slice(64 * hh, 64 * hh + 64)
                            last = mm(out, qkT[rows, qb, tt * P:(tt + 1) * P], qkT[rows, kb, :], True, True)
                last.then_inc(scores_ready, 1)

            def turn_probs(u):
                pe.wait_ge(probs_ready, u + 1)
                if u == 0:
                    pe.wait_ge(t5_copied, 1)
                else:
                    pe.wait_ge(pT_dve, u)
                    pe.wait_ge(pT_act, u)
                for hh in range(2):
                    for kt in range(T):
                        for tt in range(T):
                            last = nc.tensor.transpose(ps[:, 6 + hh, kt * S + tt * P:kt * S + (tt + 1) * P],
                                                       scores[:, u % 4, hh, tt, kt * P:(kt + 1) * P], ident[:])
                last.then_inc(probs_turned, 1)

            def attend(u):
                kind, j, g = UNITS[u]
                o = OUTPUT_OF[u]
                pe.wait_ge(pT_dve, u + 1)
                pe.wait_ge(pT_act, u + 1)
                if o >= 2:
                    pe.wait_ge(out_evac, o - 1)
                for kt in range(T):
                    for hh in range(2):
                        rhs = pT[:, u % 2, hh, kt, :]
                        if kind == "C":
                            continue
                        _, _, vc = unit_blocks(u)
                        last = mm(ps[64 * hh:64 * hh + 64, 4 + o % 2, 0:S], v[:, kt, vc + 64 * hh:vc + 64 * hh + 64], rhs,
                                  kt == 0 and g == 0, kt == T - 1 and (kind == "A" or g == 2))
                if kind == "C":
                    for hh in range(2):
                        for kt in range(T):
                            h = 2 * j + hh
                            last = mm(ps[:, 4 + o % 2, hh * S:(hh + 1) * S], mv[:, kt, h * P:(h + 1) * P],
                                      pT[:, u % 2, hh, kt, :], kt == 0, kt == T - 1)
                last.then_inc(pv_done, 1)

            def turn_x1(s):
                pe.wait_ge(front_evac, OUT0 + s + 1)
                for k in range(2):
                    for tt in range(T):
                        last = nc.tensor.transpose(ps[:, 2 + s, k * S + tt * P:k * S + (tt + 1) * P],
                                                   x[:, tt, (2 * s + k) * P:(2 * s + k + 1) * P], ident[:])
                last.then_inc(x1_turned, 1)

            def router_part(s):
                pe.wait_ge(x1T_dve if s % 2 else x1T_act, s // 2 + 1)
                for k in range(2):
                    last = mm(ps[32 * s:32 * s + EXPERTS, 6, 0:S], rw[:, 2 * s + k, :], x1T[:, 2 * s + k, :], k == 0, k == 1)
                return last

            for i, (kind, n) in enumerate(FRONT):
                if i == 0:
                    pe.wait_ge(hT_act, 4)
                    pe.wait_ge(hT_dve, 4)
                if i == 2:
                    pe.wait_ge(gcols_ok, 1)
                    turn(xn, 1, 4)
                if i == 4:
                    pe.wait_ge(hT_act, 8)
                    pe.wait_ge(hT_dve, 8)
                    pe.wait_ge(t5_in_done, 48)
                    mm(ps[0:DIL_HEADS, 7, :], t5_in[:], onehot[:], True, True).then_inc(t5_ps, 1)
                front_landed(pe, i)
                chunk = ring[:, i % FRONT_RING, :]
                prev_y = i and FRONT[i - 1][0].startswith("branch")
                if kind in ("mem", "in"):
                    if i >= 2:
                        pe.wait_ge(front_evac, i if prev_y else i - 1)
                    chunk = chunk.rearrange("p (k c) -> p k c", k=KC)
                    src = mT if kind == "mem" else hT
                    if (kind == "mem" and n < 2) or (kind == "in" and n in QKT):
                        for b in range(2):
                            for k in range(KC):
                                last = mm(ps[:, i % 2, b * S:(b + 1) * S], chunk[:, k, b * P:(b + 1) * P], src[:, k, :],
                                          k == 0, k == KC - 1)
                    else:
                        for tt in range(T):
                            for k in range(KC):
                                last = mm(ps[:, i % 2, tt * S:(tt + 1) * S], src[:, k, tt * P:(tt + 1) * P], chunk[:, k, :],
                                          k == 0, k == KC - 1)
                elif kind == "out":
                    if i == OUT0:
                        pe.wait_ge(hT_act, 12)
                        pe.wait_ge(hT_dve, 12)
                    pe.wait_ge(front_evac, i if prev_y else i - 1)
                    chunk = chunk.rearrange("p (k c) -> p k c", k=KC)
                    for tt in range(T):
                        for k in range(KC):
                            last = mm(ps[:, i % 2, tt * S:(tt + 1) * S], hT[:, k, tt * P:(tt + 1) * P], chunk[:, k, :],
                                      k == 0, k == KC - 1)
                else:
                    pe.wait_ge(front_evac, i)
                    pe.wait_ge(out_evac, {"branch_a": 6, "branch_c": 2, "branch_b": 8}[kind])
                    first = {"branch_a": 0, "branch_c": 20, "branch_b": 8}[kind]
                    halves, kc = (2, 2) if kind == "branch_b" else (1, 4)
                    chunk = chunk.rearrange("p (k h c) -> p k h c", k=kc, h=halves)
                    for half in range(halves):
                        for tt in range(T):
                            for k in range(kc):
                                last = mm(ps[:, 2 * half + tt, :], qkT[:, first + k, tt * P:(tt + 1) * P],
                                          chunk[:, k, half, :], k == 0, k == kc - 1)
                last.then_inc(chunk_used, 1)
                if i > OUT0:
                    turn_x1(i - OUT0 - 1)
                if i in STEP_AFTER:
                    s = STEP_AFTER[i]
                    if s < NU:
                        head_scores(s)
                    if 0 <= s - TURN_LAG < NU:
                        turn_probs(s - TURN_LAG)
                    if 0 <= s - PV_LAG < NU:
                        attend(s - PV_LAG)
                if kind == "branch_b":
                    for half in range(2):
                        pe.wait_ge(merged_ready, half + 1)
                        for k in range(4 * half, 4 * half + 4):
                            for tt in range(T):
                                last = nc.tensor.transpose(ps[:, 4 + k // 2, (k % 2) * S + tt * P:(k % 2) * S + (tt + 1) * P],
                                                           xn[:, tt, k * P:(k + 1) * P], ident[:])
                            if k % 2:
                                last.then_inc(turned, 1)

            turn_x1(3)
            pe.wait_ge(consts_in, 80)
            for c in range(4):
                last = router_part(c)
            last.then_inc(parts_ps, 1)
            pe.wait_ge(parts_in, 1)
            for tt in range(T):
                last = mm(ps[:, 7, 128 + tt * EXPERTS:128 + (tt + 1) * EXPERTS], router_parts[:, tt * P:(tt + 1) * P], stack4[:],
                          True, True)
            last.then_inc(router_ps, 1)
            pe.wait_ge(mask_ready, 1)
            mm(ps[:, 7, 0:EXPERTS], earlier[:], mask[:, 0, :], True, True)
            mm(ps[:, 7, 32:32 + EXPERTS], ones[:], mask[:, 0, :], True, False)
            mm(ps[:, 7, 32:32 + EXPERTS], earlier[:], mask[:, 1, :], False, True)
            mm(ps[:, 7, 64:64 + EXPERTS], ones[:], mask[:, 0, :], True, False)
            mm(ps[:, 7, 64:64 + EXPERTS], ones[:], mask[:, 1, :], False, True).then_inc(rank_ps, 1)
            def gather_half(half, width, bank=3):
                for k in range(4):
                    for tt in range(T):
                        last = mm(ps[:, bank, k * P:k * P + width], xn[:, tt, (4 * half + k) * P:(4 * half + k + 1) * P],
                                  P_pair[:, tt, 0:width], tt == 0, tt == T - 1)
                last.then_inc(gathered, 1)

            def scatter():
                for tt in range(T):
                    for hn in range(2):
                        last = mm(ps[:, 4 + 2 * tt + hn, :], WT_of[0][64 * hn:64 * hn + 64, tt * P:(tt + 1) * P],
                                  y_sb[64 * hn:64 * hn + 64, :], False, False, skip_group_check=True)
                last.then_inc(scattered, 1)

            WT_of = [WT[:, 1, :]]

            def expert(n, c, fills, wt_slot, bias_slot, bias_fill, xt, xt_fill, gather):
                def slot(j):
                    return ring_slot(c + j)

                def chunk_landed(j):
                    pe.wait_ge(landed[slot(j)], (fills + ((c + j) // RING + 1 + front_fills(slot(j)))) * 16)

                pe.wait_ge(brow_in[bias_slot], bias_fill)
                pe.wait_ge(gu_drained, n + 1)
                for b in range(2):
                    for h in range(2):
                        mm(ps[64 * h:64 * h + 64, b, :], ones[64 * bias_slot:64 * bias_slot + 1, 0:BLK],
                           brow[64 * bias_slot:64 * bias_slot + 1, b * D + 512 * h:b * D + 512 * (h + 1)], True, False)
                for k in range(KC):
                    chunk_landed(k)
                    for b in range(2):
                        for h in range(2):
                            last = mm(ps[64 * h:64 * h + 64, b, :], xt[:, k, :],
                                      ring[:, slot(k), b * D + 512 * h:b * D + 512 * (h + 1)], False, k == KC - 1)
                    last.then_inc(chunk_used, 1)
                    if k == 3:
                        pe.wait_ge(y_ready, n + 1)
                        scatter()
                        WT_of[0] = WT[:, wt_slot, :]
                        pe.wait_ge(PW_ready, n + 1)
                        for tt in range(T):
                            last = nc.tensor.transpose(ps[:, 3, tt * P:(tt + 1) * P], PW[:, tt, :], ident[:])
                        last.then_inc(WT_ps, 1)
                gather()
                pe.wait_ge(act_ready, n + 1)
                for f in range(4):
                    last = nc.tensor.transpose(ps[:, 2, f * P:(f + 1) * P], sig[:, f * P:(f + 1) * P], ident[:])
                last.then_inc(aT_ps, 1)
                pe.wait_ge(aT_ready, n + 1)
                pe.wait_ge(XT_ready, xt_fill)
                for j in range(KC, EXPERT_CHUNKS):
                    chunk_landed(j)
                    for kk in range(2):
                        k = 2 * (j - KC) + kk
                        for hn in range(2):
                            last = mm(ps[64 * hn:64 * hn + 64, 3, :], aT[:, k % 4, BLK * (k // 4):BLK * (k // 4) + BLK],
                                      ring[:, slot(j), kk * D + 512 * hn:kk * D + 512 * (hn + 1)],
                                      k == 0, k == KC - 1)
                    last.then_inc(chunk_used, 1)

            pe.wait_ge(P_ready, 1)
            pe.wait_ge(normed, 3)
            gather_half(0, 2 * BLK)
            gather_half(1, 2 * BLK, 2)
            pe.wait_ge(wsel_ready, 1)
            for tt in range(T):
                last = nc.tensor.transpose(ps[0:EXPERTS, 1, tt * P:(tt + 1) * P], w_sel[:, tt, :], ident[:])
            last.then_inc(wT_ps, 1)
            pe.wait_ge(wT_ok, 1)
            pe.wait_ge(late_in, 48)
            for tt in range(T):
                for hn in range(2):
                    last = mm(ps[:, 4 + 2 * tt + hn, :], wT_sel[:, tt * P:(tt + 1) * P], b_dn[:, 512 * hn:512 * (hn + 1)],
                              True, False, skip_group_check=True)
            last.then_inc(WT_ps, 1)
            with pe.Fori(0, EXPERTS // 4) as it:
                for q in range(4):
                    n = it * 4 + q

                    def gather():
                        pe.wait_ge(P_ready, it * 2 + (q // 2 + 2))
                        pe.wait_ge(WT_ready, n + 1)
                        gather_half(q % 2, 2 * BLK)

                    if q % 2 == 0:
                        pe.wait_ge(XT_ready, n + 2)
                    expert(n, EXPERT_CHUNKS * q, it * 3, q % 2, q % 2, (it * 2 + (q // 2 + 1)) * 16,
                           XT[:, q // 2, :, BLK * (q % 2):BLK * (q % 2) + BLK], n + 3, gather)
            n_over = pe.value_load(ovf[0:1, MAX_OVERFLOW:MAX_OVERFLOW + 1], min_val=0, max_val=MAX_OVERFLOW)
            with pe.If(0 < n_over):
                with pe.Fori(0, MAX_OVERFLOW) as b:
                    with pe.If(b < n_over):
                        n = b + EXPERTS
                        pe.wait_ge(P_ready, b + (EXPERTS // 2 + 2))
                        pe.wait_ge(y_ready, n + 1)
                        for half in range(2):
                            pe.wait_ge(XT_ready, b * 2 + (EXPERTS + 2 + half))
                            gather_half(half, BLK)
                        pe.wait_ge(XT_ready, b * 2 + (EXPERTS + 4))
                        WT_of[0] = WT[:, 1, :]
                        expert(n, 0, b + EXPERTS * EXPERT_CHUNKS // RING, 1, 0, (b + (EXPERTS // 2 + 1)) * 16, XT[:, 0, :, 0:BLK], b * 2 + (EXPERTS + 4),
                               lambda: pe.wait_ge(WT_ready, n + 1))
            pe.wait_ge(y_ready, EXPERTS + 1)
            with pe.If(0 < n_over):
                pe.wait_ge(y_ready, n_over + (EXPERTS + 1))
            WT_of[0] = WT[:, 1, :]
            scatter()

        @block.scalar
        def _(act):
            def square_sums(src, junk, m, before=None):
                for tt in range(T):
                    last = nc.scalar.activation(junk[:, tt, :], src[:, tt, :], ACT.Square, accum_out=sumsq[:, m, tt:tt + 1])
                last.then_inc(sq_done, 1)
                act.wait_ge(sq_done, (m if before is None else before - 1) + 1)
                nc.scalar.activation(rstd[:, m, :], sumsq[:, m, :], ACT.Sqrt, scale=1.0 / D, bias=eps[:, 0:1]
                                     ).then_inc(std_ready, 1)

            def hT_evac(dst, turn_no, gain):
                for k in (2, 3, 6, 7):
                    act.wait_ge(turned, 4 * turn_no + k // 2 + 1)
                    bank = {0: 0, 1: 4, 2: 4, 3: 2}[turn_no] + k // 2
                    src = ps[:, bank, (k % 2) * S:(k % 2 + 1) * S]
                    if gain is None:
                        i = nc.scalar.copy(dst[:, k, :], src)
                    else:
                        i = nc.scalar.mul(dst[:, k, :], src, g_cols[:, gain * KC + k:gain * KC + k + 1])
                    i.then_inc(hT_act, 1)

            act.wait_ge(eps_ready, 1)
            act.wait_ge(mem_in, 16)
            square_sums(mem_raw, mem_n, 0)
            act.wait_ge(x_in, 16)
            square_sums(x, xn, 1)
            act.wait_ge(gcols_ok, 1)
            hT_evac(mT, 0, 0)

            def exps(u):
                kind, j, g = UNITS[u]
                o = OUTPUT_OF[u]
                act.wait_ge(max_ready, o + 1)
                for hh in range(2):
                    for tt in range(T):
                        p = scores[:, u % 4, hh, tt, :]
                        last = nc.scalar.activation(p, p, ACT.Exp, bias=neg_max[:, o, 2 * hh + tt:2 * hh + tt + 1],
                                                    accum_out=exp_sum[:, u, 2 * hh + tt:2 * hh + tt + 1])
                last.then_inc(exp_done, 1)

            for i, (kind, n) in enumerate(FRONT):
                if i == 2:
                    hT_evac(hT, 1, 1)
                if kind in ("mem", "in"):
                    act.wait_ge(chunk_used, i + 1)
                    if kind == "in" and n in GATE_BRANCH:
                        act.wait_ge(t5_saved, 16)
                    src = ps[:, i % 2, :].rearrange("p (t c) -> p t c", t=2)
                    if kind == "mem":
                        if n < 2:
                            e = nc.scalar.copy(mkT[:, 2 * n:2 * n + 2, :], src)
                        else:
                            e = nc.scalar.copy(mv[:, :, (n - 2) * 256:(n - 1) * 256], src)
                    elif n in Q_SCALE and n < 15:
                        e = nc.scalar.mul(qkT[:, QKT[n]:QKT[n] + 2, :].rearrange("p b (t q) -> p b t q", t=T),
                                          reversed_tiles(src), Q_SCALE[n])
                    elif n in QKT:
                        e = nc.scalar.mul(qkT[:, QKT[n]:QKT[n] + 2, :], src, Q_SCALE.get(n, 1.0))
                    elif n in V_COL:
                        e = nc.scalar.copy(v[:, :, V_COL[n]:V_COL[n] + 256], src)
                    else:
                        buf, c = GATE_BRANCH[n]
                        e = nc.scalar.activation(gates[:, buf, :, c * 256:(c + 1) * 256], src, ACT.Sigmoid)
                    e.then_inc(front_evac, 1)
                if i in STEP_AFTER:
                    s = STEP_AFTER[i]
                    u = s - TURN_LAG
                    if 0 <= u < NU:
                        act.wait_ge(probs_turned, u + 1)
                        if u >= 2:
                            act.wait_ge(pv_done, u - 1)
                        nc.scalar.copy(pT[:, u % 2, 1], ps[:, 7, :].rearrange("p (k q) -> p k q", k=2)).then_inc(pT_act, 1)
                    if s < NU and s == last_unit_of(OUTPUT_OF[s]):
                        for w in range(NU):
                            if OUTPUT_OF[w] == OUTPUT_OF[s]:
                                exps(w)
                    u = s - PV_LAG
                    if 0 <= u < NU and u == last_unit_of(OUTPUT_OF[u]):
                        kind_u, j, g = UNITS[u]
                        o = OUTPUT_OF[u]
                        act.wait_ge(pv_done, u + 1)
                        if kind_u == "C":
                            e = nc.scalar.copy(qkT[:, 20 + 2 * j:22 + 2 * j, :],
                                               ps[:, 4 + o % 2, :].rearrange("p (h q) -> p h q", h=2))
                        else:
                            e = nc.scalar.copy(qkT[:, j + (8 if kind_u == "B" else 0), :].rearrange("p (t q) -> p t q", t=T),
                                               reversed_tiles(ps[:, 4 + o % 2, 0:S]))
                        e.then_inc(out_evac, 1)
            hT_evac(hT, 2, None)
            for c in range(4):
                if c < 3:
                    act.wait_ge(front_evac, OUT0 + c + 1)
                    if c:
                        act.wait_ge(square_parts, c)
                    for tt in range(T):
                        last = nc.scalar.activation(sq_tmp[:, tt, :], x[:, tt, c * SLOTS_W:(c + 1) * SLOTS_W], ACT.Square,
                                                    accum_out=part_sums[:, tt, c:c + 1])
                    last.then_inc(square_parts, 1)
                if c % 2 == 0:
                    act.wait_ge(x1_turned, c + 1)
                    for k in (2 * c, 2 * c + 1):
                        last = nc.scalar.mul(x1T[:, k, :], ps[:, 2 + c, (k % 2) * S:(k % 2 + 1) * S],
                                             g_cols[:, 2 * KC + k:2 * KC + k + 1])
                    last.then_inc(x1T_act, 1)
                if c == 2:
                    nc.scalar.activation(sumsq[:, 3, 0:1], eps[:], ACT.Sqrt)
            act.wait_ge(sums_ready, 1)
            nc.scalar.activation(rstd[:, 2, :], sumsq[:, 2, :], ACT.Sqrt, scale=1.0 / D, bias=eps[:, 0:1]).then_inc(std_ready, 1)
            act.wait_ge(top_ready, 1)
            for tt in range(T):
                last = nc.scalar.activation(prob[:, tt, :], logits[:, tt, 0:EXPERTS], ACT.Exp, bias=neg_top[:, tt:tt + 1])
            last.then_inc(probs_exp, 1)

            def move_gathered(half, xt, width, count_before, bank=3):
                act.wait_ge(gathered, count_before + 1)
                for k in range(4):
                    c = 4 * half + k
                    last = nc.scalar.mul(xt[:, c, 0:width], ps[:, bank, k * P:k * P + width],
                                         g_cols[:, 2 * KC + c:2 * KC + c + 1])
                last.then_inc(XT_ready, 1)

            for half in range(2):
                move_gathered(half, XT[:, 0], 2 * BLK, half, 3 - half)

            def expert(n, wt_slot, gathered_next):
                act.wait_ge(WT_ps, n + 2)
                nc.scalar.copy(WT[:, wt_slot, :], ps[:, 3, 0:S]).then_inc(WT_ready, 1)
                act.wait_ge(gate_ready, n + 1)
                nc.scalar.activation(sig, gate_c, ACT.Sigmoid, scale=ALPHA).then_inc(sig_ready, 1)
                gathered_next()
                act.wait_ge(chunk_used, NF + EXPERT_CHUNKS * (n + 1))
                nc.scalar.copy(y_sb, ps[:, 3, :]).then_inc(y_ready, 1)

            with act.Fori(0, EXPERTS // 4) as it:
                for q in range(4):
                    n = it * 4 + q
                    expert(n, q % 2, lambda: move_gathered(q % 2, XT[:, (q // 2 + 1) % 2], 2 * BLK, n + 2))
            n_over = act.value_load(ovf[0:1, MAX_OVERFLOW:MAX_OVERFLOW + 1], min_val=0, max_val=MAX_OVERFLOW)
            with act.If(0 < n_over):
                with act.Fori(0, MAX_OVERFLOW) as b:
                    with act.If(b < n_over):
                        for half in range(2):
                            move_gathered(half, XT[:, 0], BLK, b * 2 + (EXPERTS + 2 + half))
                        expert(b + EXPERTS, 1, lambda: None)
            act.wait_ge(x1_ready, 1)
            square_sums(x, final, 3, 3)

        @block.vector
        def _(dve):
            vec = nc.vector
            links = [0]

            def link(i):
                links[0] += 1
                i.then_inc(dve_chain, 1)
                dve.wait_ge(dve_chain, links[0])

            def normalise(src, dst, m):
                dve.wait_ge(std_ready, m + 1)
                link(vec.reciprocal(rstd[:, m, :], rstd[:, m, :]))
                for tt in range(T):
                    last = vec.tensor_scalar(dst[:, tt, :], src[:, tt, :], rstd[:, m, tt:tt + 1], None, ALU.mult)
                last.then_inc(normed, 1)

            def hT_evac(dst, turn_no, gain):
                for k in (0, 1, 4, 5):
                    dve.wait_ge(turned, 4 * turn_no + k // 2 + 1)
                    bank = {0: 0, 1: 4, 2: 4, 3: 2}[turn_no] + k // 2
                    src = ps[:, bank, (k % 2) * S:(k % 2 + 1) * S]
                    if gain is None:
                        i = vec.tensor_copy(dst[:, k, :], src)
                    else:
                        i = vec.tensor_scalar(dst[:, k, :], src, g_cols[:, gain * KC + k:gain * KC + k + 1], None, ALU.mult)
                    i.then_inc(hT_dve, 1)

            vec.memset(eps[:], EPS).then_inc(eps_ready, 1)
            link(vec.memset(ones[:], 1.0))
            dve.wait_ge(gcols_ps, 1)
            vec.tensor_copy(g_cols[:, 0:3 * KC], ps[:, 6, 0:3 * KC]).then_inc(gcols_ok, 1)
            normalise(mem_raw, mem_n, 0)
            normalise(x, xn, 1)
            dve.wait_ge(gcols_ok, 1)
            hT_evac(mT, 0, 0)
            hT_evac(hT, 1, 1)
            dve.wait_ge(t5_ps, 1)
            vec.tensor_copy(t5_rows, ps[0:DIL_HEADS, 7, :]).then_inc(t5_copied, 1)

            for i, (kind, n) in enumerate(FRONT):
                if kind.startswith("branch"):
                    dve.wait_ge(chunk_used, i + 1)
                    dve.wait_ge(front_evac, i)
                    for half in range(2 if kind == "branch_b" else 1):
                        lo = 512 * (half if kind == "branch_b" else n)
                        y = ps[:, 2 * half:2 * half + 2, :]
                        m = xn[:, :, lo:lo + 512]
                        g = gates[:, 1 if kind == "branch_c" else 0, :, lo:lo + 512]
                        if kind == "branch_a":
                            last = vec.tensor_tensor(m, g, y, ALU.mult)
                        else:
                            link(vec.tensor_tensor(g, g, y, ALU.mult))
                            last = vec.tensor_tensor(m, m, g, ALU.add)
                            if kind == "branch_b":
                                last.then_inc(merged_ready, 1)
                    if kind == "branch_b":
                        dve.wait_ge(merged_ready, 2)
                        last = vec.memset(b_tmp[:], 0.0)
                    last.then_inc(front_evac, 1)
                if kind == "out":
                    dve.wait_ge(chunk_used, i + 1)
                    xs = x[:, :, n * SLOTS_W:(n + 1) * SLOTS_W]
                    vec.tensor_tensor(xs, xs, ps[:, i % 2, :].rearrange("p (t c) -> p t c", t=2), ALU.add
                                      ).then_inc(front_evac, 1)
                    if n in (1, 3):
                        if n == 3:
                            dve.wait_ge(front_evac, NF)
                            dve.wait_ge(square_parts, 3)
                            link(vec.tensor_tensor(sq_tmp, xs, xs, ALU.mult))
                            link(vec.tensor_reduce(part_sums[:, :, 3], sq_tmp, AX_X, ALU.add))
                            vec.tensor_reduce(sumsq[:, 2, :], part_sums, AX_X, ALU.add).then_inc(sums_ready, 1)
                        dve.wait_ge(x1_turned, n + 1)
                        for k in (2 * n, 2 * n + 1):
                            last = vec.tensor_scalar(x1T[:, k, :], ps[:, 2 + n, (k % 2) * S:(k % 2 + 1) * S],
                                                     g_cols[:, 2 * KC + k:2 * KC + k + 1], None, ALU.mult)
                        last.then_inc(x1T_dve, 1)
                if i in STEP_AFTER:
                    s = STEP_AFTER[i]
                    if s < NU:
                        kind_u, j, g = UNITS[s]
                        dve.wait_ge(scores_ready, s + 1)
                        if s >= 4:
                            dve.wait_ge(probs_turned, s - 3)
                        if kind_u != "C":
                            b = (s - 2) % 4
                            dve.wait_ge(image_in[b], 16 * ((s - 2) // 4 + 1))
                            if kind_u == "A":
                                im = image[:, b].rearrange("p h (r c) -> p (h r) c", c=GRID_W)
                                link(vec.tensor_tensor(im, im, bcast(na_mask[:], 1, 2 * IMG // GRID_W), ALU.add))
                        for tt in range(T):
                            src = ps[:, 2:4, tt * S:(tt + 1) * S]
                            dst = scores[:, s % 4, :, tt, :]
                            if kind_u == "C":
                                last = vec.tensor_copy(dst, src)
                            else:
                                last = vec.tensor_tensor(dst, src, image[:, b, :, P - P * tt:P - P * tt + S], ALU.add)
                        last.then_inc(scores_drained, 1)
                        dve.wait_ge(scores_drained, s + 1)
                        link(vec.tensor_reduce(row_max[:, s, :], scores[:, s % 4].rearrange("p h t k -> p (h t) k"),
                                               AX_X, ALU.max))
                        o = OUTPUT_OF[s]
                        if s == last_unit_of(o):
                            if kind_u == "B":
                                link(vec.tensor_tensor(b_tmp[:, 0, :], row_max[:, s - 2, :], row_max[:, s - 1, :], ALU.max))
                                link(vec.tensor_tensor(row_max[:, s, :], b_tmp[:, 0, :], row_max[:, s, :], ALU.max))
                            vec.tensor_scalar(neg_max[:, o, :], row_max[:, s, :], -1.0, None, ALU.mult).then_inc(max_ready, 1)
                    u = s - TURN_LAG
                    if 0 <= u < NU:
                        dve.wait_ge(probs_turned, u + 1)
                        if u >= 2:
                            dve.wait_ge(pv_done, u - 1)
                        vec.tensor_copy(pT[:, u % 2, 0], ps[:, 6, :].rearrange("p (k q) -> p k q", k=2)).then_inc(pT_dve, 1)
                    if s < NU and s == last_unit_of(OUTPUT_OF[s]):
                        o = OUTPUT_OF[s]
                        dve.wait_ge(exp_done, s + 1)
                        total = exp_sum[:, s, :]
                        if UNITS[s][0] == "B":
                            link(vec.tensor_tensor(b_tmp[:, 0, :], exp_sum[:, s - 2, :], exp_sum[:, s - 1, :], ALU.add))
                            link(vec.tensor_tensor(b_tmp[:, 1, :], b_tmp[:, 0, :], exp_sum[:, s, :], ALU.add))
                            total = b_tmp[:, 1, :]
                        link(vec.reciprocal(inv_sum[:, o, :], total))
                        for w in range(NU):
                            if OUTPUT_OF[w] == o:
                                p = scores[:, w % 4].rearrange("p h t k -> p (h t) k")
                                vec.tensor_tensor(p, p, bcast(inv_sum[:, o, :], 2, S), ALU.mult).then_inc(probs_ready, 1)
                if kind == "branch_b":
                    hT_evac(hT, 2, None)
            link(vec.memset(logits[:, :, EXPERTS:], SENTINEL))
            link(vec.memset(keys[:, :, EXPERTS:], -NO_SLOT))
            vec.memset(b_tmp[:], 0.0).then_inc(gu_drained, 1)
            dve.wait_ge(std_ready, 3)
            vec.reciprocal(rstd[:, 2, :], rstd[:, 2, :]).then_inc(rstd_ready, 1)
            dve.wait_ge(parts_ps, 1)
            vec.tensor_copy(router_parts, ps[:, 6, 0:S]).then_inc(parts_in, 1)
            dve.wait_ge(rstd_ready, 1)
            dve.wait_ge(router_ps, 1)
            for tt in range(T):
                link(vec.scalar_tensor_tensor(logits[:, tt, 0:EXPERTS], ps[:, 7, 128 + tt * EXPERTS:128 + (tt + 1) * EXPERTS],
                                              rstd[:, 2, tt:tt + 1], rb[:], ALU.mult, ALU.add))
            for tt in range(T):
                link(vec.max(top8[:, tt, :], logits[:, tt, :]))
            vec.tensor_scalar(neg_top, top8[:, :, 0], -1.0, None, ALU.mult).then_inc(top_ready, 1)
            link(vec.memset(top8[:, :, TOP_K:], SENTINEL))
            for tt in range(T):
                link(vec.match_replace(replaced[:, tt, :], top8[:, tt, :], logits[:, tt, :], REPLACED))
            vec.tensor_tensor(mask, replaced[:, :, 0:EXPERTS], logits[:, :, 0:EXPERTS], ALU.not_equal).then_inc(mask_ready, 1)
            dve.wait_ge(mask_ready, 1)
            dve.wait_ge(probs_exp, 1)
            link(vec.tensor_tensor(prob_m, prob, mask, ALU.mult))
            link(vec.tensor_reduce(w_sum, prob_m, AX_X, ALU.add))
            link(vec.reciprocal(w_inv, w_sum))
            vec.tensor_tensor(w_sel, prob_m, bcast(w_inv, 2, EXPERTS), ALU.mult).then_inc(wsel_ready, 1)
            vec.memset(WT[:, 1, :], 0.0)
            vec.memset(y_sb, 0.0).then_inc(y_ready, 1)
            dve.wait_ge(rank_ps, 1)
            link(vec.tensor_scalar(tmp_a, mask, NO_SLOT, -NO_SLOT, ALU.mult, ALU.add))
            link(vec.tensor_tensor(keys[:, :, 0:EXPERTS], tmp_a, ps[:, 7, 0:T * EXPERTS].rearrange("p (t e) -> p t e", t=T),
                                   ALU.add))
            link(vec.tensor_copy(count, ps[:, 7, 64:64 + EXPERTS]))

            def gather_matrix(col, width, slots):
                for tt in range(T):
                    last = vec.tensor_scalar(P_pair[:, tt, col:col + width], slots, keys_at[0][:, tt, keys_at[1]], None,
                                             ALU.is_equal)
                return last

            keys_at = [keys, slice(0, 1)]
            dve.wait_ge(late_in, 48)
            gather_matrix(0, BLK, iota[:, 0:BLK])
            keys_at[1] = slice(1, 2)
            gather_matrix(BLK, BLK, iota[:, 0:BLK]).then_inc(P_ready, 1)
            dve.wait_ge(wT_ps, 1)
            vec.tensor_copy(wT_sel, ps[0:EXPERTS, 1, 0:S]).then_inc(wT_ok, 1)
            link(vec.tensor_scalar(extra, count, float(BLK), None, ALU.is_gt))
            for lim in (2 * BLK, 3 * BLK):
                link(vec.tensor_scalar(tmp_a[:, 0, :], count, float(lim), None, ALU.is_gt))
                link(vec.tensor_tensor(extra, extra, tmp_a[:, 0, :], ALU.add))
            link(vec.tensor_tensor_scan(ends, extra, extra, 0.0, ALU.add, ALU.bypass))
            link(vec.tensor_tensor(tmp_a[:, 0, :], ends, extra, ALU.subtract))
            link(vec.tensor_scalar(tmp_a[:, 0, :], tmp_a[:, 0, :], float(BLK), NO_SLOT - BLK, ALU.mult, ALU.add))
            link(vec.tensor_tensor(okeys, keys[:, :, 0:EXPERTS], bcast(tmp_a[:, 0, :], 1, T), ALU.add))
            link(vec.tensor_scalar(tmp_b, keys[:, :, 0:EXPERTS], float(BLK), None, ALU.is_ge))
            link(vec.tensor_tensor(okeys, okeys, tmp_b, ALU.mult))
            link(vec.tensor_scalar(okeys, okeys, NO_SLOT, None, ALU.subtract))
            link(vec.tensor_tensor(ends_le, bcast(ends, 1, MAX_OVERFLOW), bcast(iota[:, 0:MAX_OVERFLOW], 2, EXPERTS), ALU.is_le))
            link(vec.tensor_reduce(ovf_f, ends_le, AX_X, ALU.add))
            link(vec.tensor_scalar(ovf_f, ovf_f, float(EXPERTS - 1), None, ALU.min))
            link(vec.tensor_copy(ovf[:, 0:MAX_OVERFLOW], ovf_f))
            vec.tensor_copy(ovf[:, MAX_OVERFLOW:], ends[:, EXPERTS - 1:EXPERTS]).then_inc(routed, 1)

            def expert(n, key_tile, slots, e):
                dve.wait_ge(WT_ps, n + 1)
                for tt in range(T):
                    last = vec.tensor_scalar(PW[:, tt, :].rearrange("p (a s) -> p a s", a=2), bcast(slots, 1, 2),
                                             key_tile[:, tt, e], w_sel[:, tt, e], ALU.is_equal, ALU.mult)
                last.then_inc(PW_ready, 1)
                dve.wait_ge(chunk_used, NF + EXPERT_CHUNKS * n + KC)
                vec.tensor_scalar(gate_c, ps[:, 0, :], LIMIT, None, ALU.min).then_inc(gate_ready, 1)
                vec.tensor_scalar(up_c, ps[:, 1, :], -LIMIT, LIMIT, ALU.max, ALU.min).then_inc(gu_drained, 1)
                dve.wait_ge(gate_ready, n + 1)
                dve.wait_ge(gu_drained, n + 2)
                vec.scalar_tensor_tensor(up_c, up_c, 1.0, gate_c, ALU.add, ALU.mult).then_inc(prod_ready, 1)
                dve.wait_ge(prod_ready, n + 1)
                dve.wait_ge(sig_ready, n + 1)
                vec.tensor_tensor(sig, up_c, sig, ALU.mult).then_inc(act_ready, 1)
                dve.wait_ge(aT_ps, n + 1)
                vec.tensor_copy(aT, ps[:, 2, :].rearrange("p (f s) -> p f s", f=4)).then_inc(aT_ready, 1)

            with dve.Fori(0, EXPERTS // 4) as it:
                for q in range(4):
                    n = it * 4 + q
                    if q % 2 == 0:
                        dve.wait_ge(gathered, n + 2)
                        for a in range(2):
                            keys_at[1] = bass.ds(n + (2 + a), 1)
                            last = gather_matrix(BLK * a, BLK, iota[:, 0:BLK])
                        last.then_inc(P_ready, 1)
                    expert(n, keys, iota[:, 0:BLK], bass.ds(n, 1))
            dve.wait_ge(routed, 1)
            n_over = dve.value_load(ovf[0:1, MAX_OVERFLOW:MAX_OVERFLOW + 1], min_val=0, max_val=MAX_OVERFLOW)
            with dve.If(0 < n_over):
                with dve.Fori(0, MAX_OVERFLOW) as b:
                    with dve.If(b < n_over):
                        e_b = dve.value_load(ovf[0:1, bass.ds(b, 1)], min_val=0, max_val=EXPERTS - 1)
                        slots = iota[:, bass.ds(b * BLK, BLK)]
                        dve.wait_ge(gathered, b * 2 + (EXPERTS + 2))
                        keys_at[0], keys_at[1] = okeys, bass.ds(e_b, 1)
                        gather_matrix(0, BLK, slots).then_inc(P_ready, 1)
                        expert(b + EXPERTS, okeys, slots, bass.ds(e_b, 1))
            dve.wait_ge(scattered, EXPERTS + 1)
            with dve.If(0 < n_over):
                dve.wait_ge(scattered, n_over + (EXPERTS + 1))
                vec.memset(b_tmp[:], 0.0)
            y = ps[:, 4:8, :].rearrange("p (t h) c -> p t (h c)", t=T)
            vec.tensor_tensor(x[:], x[:], y, ALU.add).then_inc(x1_ready, 1)
            dve.wait_ge(x1_ready, 1)
            dve.wait_ge(std_ready, 4)
            link(vec.reciprocal(rstd[:, 3, :], rstd[:, 3, :]))
            for tt in range(T):
                last = vec.scalar_tensor_tensor(final[:, tt, :], x[:, tt, :], rstd[:, 3, tt:tt + 1], final_g,
                                                ALU.mult, ALU.mult)
            last.then_inc(final_ready, 1)


def t5_bucket(rel):
    half = T5_BUCKETS // 2
    exact = half // 2
    n = np.abs(rel)
    large = exact + (np.log(np.maximum(n, 1).astype(np.float32) / exact) / math.log(T5_MAX_DIST / exact)
                     * (half - exact)).astype(np.int32)
    return np.where(rel > 0, half, 0) + np.where(n < exact, n, np.minimum(large, half - 1))


def constants():
    rel = np.arange(REL) - (S - 1)
    onehot = np.zeros((T5_BUCKETS + 3, REL), np.float32)
    onehot[t5_bucket(rel), np.arange(REL)] = 1.0
    for g, (dil, window) in enumerate(zip(DIL, DIL_WINDOW)):
        ok = (rel % dil == 0) & (np.abs(rel) // dil <= window // 2 // dil)
        onehot[T5_BUCKETS + g] = np.where(ok, 0.0, NEG)
    group = np.zeros((3, DIL_HEADS), np.float32)
    for g in range(3):
        group[g, g * GROUP_HEADS:(g + 1) * GROUP_HEADS] = 1.0
    col = np.arange(GRID_W)
    start = np.clip(col - WIN_COLS // 2, 0, GRID_W - WIN_COLS)
    ok = (col[None] >= start[:, None]) & (col[None] < start[:, None] + WIN_COLS)
    na_mask = np.tile(np.where(ok, 0.0, NEG).astype(np.float32), (P // GRID_W, 1))[::-1].copy()
    return {"bucket_onehot": onehot, "group_of_head": group, "na_mask": na_mask, "ident": np.eye(P, dtype=np.float32),
            "stack4": np.tile(np.eye(EXPERTS, dtype=np.float32), (4, 1)),
            "earlier": np.triu(np.ones((P, P), np.float32), 1), "iota": np.arange(D, dtype=np.float32)}


_DIRECT = ["x", "mem", "w_in", "w_mem_kv", "t5_rel_bias", "w_branch_a", "w_branch_b", "w_branch_c", "w_out", "router_w",
           "router_b", "expert_w_gate_up", "expert_b_gate_up", "expert_w_down", "expert_b_down", "final_norm_g"]


def kernel(**inputs):
    import concourse.bacc as bacc
    from concourse.bass_utils import run_bass_kernel_spmd

    arrays = {n: np.ascontiguousarray(inputs[n]) for n in _DIRECT}
    arrays.update(constants())
    arrays["g_rows"] = np.concatenate([np.asarray(inputs[n]).reshape(KC, P)
                                       for n in ("mem_norm_g", "attn_norm_g", "ffn_norm_g")], 0)
    rpb = np.asarray(inputs["na_rpb"])[0]
    rows = np.zeros((NA_HEADS, REL), rpb.dtype)
    dc = np.arange(-(WIN_COLS - 1), WIN_COLS)
    for dr in range(-(S // GRID_W - 1), S // GRID_W):
        rows[:, GRID_W * dr + dc + S - 1] = rpb[:, dr + WIN_ROWS - 1, :]
    arrays["na_rows"] = rows
    nc = bacc.Bacc("TRN2", target_bir_lowering=False, num_devices=1)
    t = {n: nc.dram_tensor(f"in_{n}", a.shape, mybir.dt.from_np(a.dtype), kind="ExternalInput").ap()
         for n, a in arrays.items()}
    t["out"] = nc.dram_tensor("out_0", (1, S, D), F32, kind="ExternalOutput").ap()
    build(nc, t)
    r = run_bass_kernel_spmd(nc, [{f"in_{n}": a for n, a in arrays.items()}], core_ids=[0])
    return np.asarray(r.results[0]["out_0"])
```

```python
import math
from contextlib import ExitStack

import numpy as np
import concourse.bass as bass
from concourse import mybir

F32 = mybir.dt.float32
F32R = mybir.dt.float32r
I32 = mybir.dt.int32
ALU = mybir.AluOpType
ACT = mybir.ActivationFunctionType
AX_X = mybir.AxisListType.X

P = 128
D = 1024
KC = D // P
S = 256
T = S // P
MEM = 256
GRID_W, WIN_COLS, WIN_ROWS = 64, 16, 8
NA_HEADS, HD = 8, 64
DIL = (1, 4, 16)
DIL_WINDOW = (128, 512, 2048)
GROUP_HEADS = 4
DIL_HEADS = GROUP_HEADS * len(DIL)
MEM_HEADS, MEM_HD = 4, 128
T5_BUCKETS, T5_MAX_DIST = 32, 1024
EXPERTS, TOP_K = 32, 4
ALPHA, LIMIT, EPS = 1.702, 7.0, 1e-6
NEG = -1e30
SENTINEL = -3e38
REPLACED = -3.2e38
NO_SLOT = 4096.0

BLK = 64
CHUNK = 2048
RING = 16
FRONT_RING = 6
SPLIT_SLOT = 6
SCORE_SLOT = 10
FRONT_SLOT = 12
FRONT_WORK = 19200
IMAGES = 3
EXPERT_CHUNKS = 12
MAX_OVERFLOW = S * TOP_K // BLK
REL = 2 * S
IMG = 3 * P
SLOTS_W = 256

FRONT = ([("mem", i) for i in range(4)] + [("in", i) for i in (15, 16)] + [("in", i) for i in range(15)]
         + [("in", i) for i in range(17, 21)]
         + [("branch_a", 0), ("in", 25), ("branch_a", 1), ("in", 26), ("in", 27), ("branch_c", 0), ("in", 28),
            ("branch_c", 1), ("in", 21), ("branch_b", 0), ("in", 22), ("in", 23), ("in", 24)]
         + [("out", i) for i in range(4)])
NF = len(FRONT)
OUT0 = NF - 4
LAST_A, ONLY_B = FRONT.index(("branch_a", 1)), FRONT.index(("branch_b", 0))
PLAIN = [sum(not kind.startswith("branch") for kind, _ in FRONT[:i]) for i in range(NF + 1)]
MERGE_BANK = (6, 7, 2, 3)
UNITS = [("C", 0, 0), ("C", 1, 0)] + [("A", j, 0) for j in range(4)] + [("B", j, g) for j in range(2) for g in range(3)]
NU = len(UNITS)
OUTPUT_OF = [0, 1, 2, 3, 4, 5, 6, 6, 6, 7, 7, 7]
TURN_LAG, PV_LAG = 3, 4
STEP_AFTER = {6: 0, 7: 1, 10: 2, 11: 3, 12: 4, 13: 5, 18: 6, 19: 7, 20: 8, 22: 9, 23: 10, 24: 11, 27: 12, 28: 13, 29: 14,
              30: 15}
T5_STORE_AFTER = 11
STEP_SLOT = {s: i for i, s in STEP_AFTER.items()}
IMAGE_AFTER = {u: 9 if u < 2 + IMAGES else STEP_SLOT[u - IMAGES] + FRONT_RING for u in range(2, NU)}
EARLY_AFTER = {36: (0, 1), 37: (2, 3), 38: (4, 5)}
EARLY = 6
QK_DONE, QKV_DONE = {"C": 6, "A": 10, "B": 18}, {"C": 6, "A": 12, "B": 21}
QKT = {0: 0, 1: 2, 2: 4, 3: 6, 6: 8, 7: 10, 8: 12, 9: 14, 10: 16, 11: 18, 15: 20, 16: 22}
V_COL = {4: 0, 5: 256, 12: 512, 13: 768, 14: 1024}
Q_SCALE = {0: HD ** -0.5, 1: HD ** -0.5, 6: HD ** -0.5, 7: HD ** -0.5, 8: HD ** -0.5,
           15: MEM_HD ** -0.5, 16: MEM_HD ** -0.5}
GATE_BRANCH = {**{i: (0, i - 17) for i in range(17, 21)}, **{i: (1, i - 25) for i in range(25, 29)},
               **{i: (0, i - 21) for i in range(21, 25)}}


def image_rows(u):
    kind, j, g = UNITS[u]
    return 2 * j if kind == "A" else NA_HEADS + g * GROUP_HEADS + 2 * j


def unit_blocks(u):
    kind, j, g = UNITS[u]
    if kind == "A":
        return j, 4 + j, 128 * j
    b = g * 2 + j
    return 8 + b, 14 + b, 512 + 128 * b


PART_PAIRS = ((0, 0), (1, 0), (0, 1))


def output_blocks(o):
    kind, j, _ = UNITS[last_unit_of(o)]
    return {"C": (20 + 2 * j, 2), "A": (j, 1), "B": (16 + j, 1)}[kind]


def last_unit_of(o):
    return max(u for u in range(NU) if OUTPUT_OF[u] == o)


def build(nc, t):
    w_in = t["w_in"].rearrange("l (k p) c -> (l p) k c", p=P)
    w_mem = t["w_mem_kv"].rearrange("l (k p) c -> (l p) k c", p=P)
    w_out = t["w_out"].rearrange("l (k p) c -> (l p) k c", p=P)
    w_br = {b: t[f"w_{b}"].rearrange("l (k p) c -> (l p) k c", p=P) for b in ("branch_a", "branch_b", "branch_c")}
    w_gu = t["expert_w_gate_up"].rearrange("l e (k p) c -> (l e) p k c", p=P)
    w_dn = t["expert_w_down"].rearrange("l e (k p) c -> (l e) p k c", p=P)
    b_gu = t["expert_b_gate_up"]
    na_rows = t["na_rows"]
    t5_scratch = nc.dram_tensor("t5_scratch", [DIL_HEADS, REL], F32, kind="Internal").ap()

    with ExitStack() as ctx:
        def sb(name, shape, dt=F32):
            return ctx.enter_context(nc.sbuf_tensor(name, shape, dt))

        def sem(name):
            return ctx.enter_context(nc.semaphore(name))

        ident = sb("ident", [P, P])
        earlier = sb("earlier", [P, P])
        ones = sb("ones", [P, P])
        na_mask = sb("na_mask", [P, GRID_W])
        g_rows = sb("g_rows", [3 * KC, P])
        g_cols = sb("g_cols", [P, 4 * KC])
        eps = sb("eps", [P, 1])
        x = sb("x_tokens", [P, T, D])
        xn = sb("x_normed", [P, T, D])
        hHL = sb("h_T_parts", [P, 2, KC, S], F32R)
        h_at = nc.sbuf_base - 2 * KC * S * 4
        rw = sb("router_w_sb", [P, KC, EXPERTS])
        rb = sb("router_b_sb", [P, EXPERTS])
        stack4 = sb("stack4", [P, EXPERTS])
        sumsq = sb("sumsq", [P, 4, T])
        rstd = sb("rstd", [P, 4, T])
        row_max = sb("row_max", [P, NU, 4])
        neg_max = sb("neg_max", [P, 8, 4])
        exp_sum = sb("exp_sum", [P, NU, 4])
        inv_sum = sb("inv_sum", [P, 8, 4])
        ovf = sb("ovf", [P, MAX_OVERFLOW + 1], I32)
        b_tmp = sb("b_tmp", [P, 2, 4])

        base = -(-nc.sbuf_base // 64) * 64
        FRONT0, MOE0 = FRONT_SLOT * CHUNK, RING * CHUNK
        arena = nc.alloc_sbuf_tensor_at("arena", [P, FRONT0 + FRONT_WORK], F32, offset=base)
        ring = arena[:, 0:RING * CHUNK].rearrange("p (r c) -> p r c", r=RING)

        def split_at(name, at, *dims):
            return nc.alloc_sbuf_tensor_at(name, [P, *dims], F32R, offset=base + 4 * at)

        def area(off, *dims):
            n = int(np.prod(dims))
            assert off + n <= FRONT0 + FRONT_WORK
            flat = arena[:, off:off + n]
            if len(dims) == 2:
                return flat.rearrange("p (a b) -> p a b", a=dims[0])
            if len(dims) == 3:
                return flat.rearrange("p (a b c) -> p a b c", a=dims[0], b=dims[1])
            if len(dims) == 4:
                return flat.rearrange("p (a b c d) -> p a b c d", a=dims[0], b=dims[1], c=dims[2])
            return flat

        image = area(FRONT0, IMAGES, 2, IMG)
        pT = area(FRONT0 + 2304, 2, 2, 2, S)
        qkT = area(FRONT0 + 4352, 24, S)
        v = area(FRONT0 + 10496, T, 1280)
        mkT = area(FRONT0 + 13056, MEM_HEADS, MEM)
        mv = area(FRONT0 + 14080, T, MEM_HEADS * MEM_HD)
        gates = area(FRONT0 + 15104, 2, T, D)
        onehot = area(FRONT0 + 10496, REL)[0:T5_BUCKETS + 3, :]
        t5_in = area(FRONT0 + 11008, DIL_HEADS)[0:T5_BUCKETS + 3, :]
        mem_raw = area(FRONT0 + 2304, T, D)
        mem_n = area(FRONT0 + 15104, T, D)
        t5_rows = area(FRONT0 + 15104, REL)[0:DIL_HEADS, :]
        scores = ring[:, SCORE_SLOT:FRONT_SLOT, :].rearrange("p a (b h t k) -> p (a b) h t k", b=2, h=2, t=2)
        wHL = split_at("w_parts", SPLIT_SLOT * CHUNK, 2, 2, CHUNK)
        qkP = split_at("attention_parts", FRONT0 + 4352, 24, S)
        mkP = split_at("memory_parts", FRONT0 + 13056, MEM_HEADS, MEM)
        mergedHL = split_at("merged_T_parts", RING * CHUNK, 2, KC, S)
        mHL = split_at("mem_T_parts", FRONT0 + 4352, 2, KC, MEM)
        XT = nc.alloc_sbuf_tensor_at("gathered_T", [P, 2, KC, 2 * BLK], F32, offset=h_at)
        place = [MOE0]

        def moe(*dims):
            at = place[0]
            place[0] += int(np.prod(dims))
            return area(at, *dims)

        brow = moe(2 * D)
        b_dn = moe(D)[0:EXPERTS, :]
        final_g = moe(D)
        iota = moe(D)
        x1T = area(place[0], KC, S)
        P_pair = moe(T, 2 * BLK)
        PW = moe(T, 2 * BLK)
        WT = moe(2, S)
        gate_c, up_c, sig = moe(512), moe(512), moe(512)
        aT = moe(4, P)
        y_sb = moe(512)
        logits, top8, replaced = moe(T, 40), moe(T, 8), moe(T, 40)
        mask, neg_top = moe(T, EXPERTS), moe(T)
        prob, prob_m, w_sum, w_inv, w_sel = moe(T, EXPERTS), moe(T, EXPERTS), moe(T), moe(T), moe(T, EXPERTS)
        keys = moe(T, EXPERTS + 4)
        okeys = moe(T, EXPERTS)
        count, extra, ends = moe(EXPERTS), moe(EXPERTS), moe(EXPERTS)
        tmp_a, tmp_b = moe(T, EXPERTS), moe(T, EXPERTS)
        ends_le = moe(MAX_OVERFLOW, EXPERTS)
        ovf_f = moe(MAX_OVERFLOW)
        wT_sel = moe(S)[0:EXPERTS, :]
        router_parts = moe(S)
        sq_tmp = aT.rearrange("p f s -> p (f s)").rearrange("p (t c) -> p t c", t=T)
        part_sums = moe(T, 4)
        final = xn[:]

        ps = ctx.enter_context(nc.psum_tensor("ps", [P, 8, 512], F32))

        landed = [sem(f"landed{i}") for i in range(RING)]
        first_in, t5_in_done, consts_in = sem("first_in"), sem("t5_in_done"), sem("consts_in")
        mem_in = [sem(f"mem_in{i}") for i in range(T)]
        x_in = sem("x_in")
        t5_saved = sem("t5_saved")
        image_in = [sem(f"image_in{i}") for i in range(IMAGES)]
        iota_in, b_dn_in, final_g_in = sem("iota_in"), sem("b_dn_in"), sem("final_g_in")
        branch_evac = sem("branch_evac")
        brow_in = [sem(f"brow_in{i}") for i in range(2)]
        out_saved = sem("out_saved")
        chunk_used = sem("chunk_used")
        gcols_ps, gcols_ok = sem("gcols_ps"), sem("gcols_ok")
        t5_ps, t5_copied = sem("t5_ps"), sem("t5_copied")
        rstd_ready, x1T_act, x1T_dve, parts_ps, parts_in, square_parts = (
            sem("rstd_ready"), sem("x1T_act"), sem("x1T_dve"), sem("parts_ps"), sem("parts_in"), sem("square_parts"))
        x1_turned = sem("x1_turned")
        high_ready, low_ready = sem("high_ready"), sem("low_ready")
        normed = sem("normed")
        turned = sem("turned")
        h_high, h_low = sem("h_high"), sem("h_low")
        sums_ready = sem("sums_ready")
        sq_done, std_ready = sem("sq_done"), sem("std_ready")
        probs_exp = sem("probs_exp")
        front_evac = sem("front_evac")
        scores_ready, scores_drained = sem("scores_ready"), sem("scores_drained")
        max_ready, exp_done, probs_ready = sem("max_ready"), sem("exp_done"), sem("probs_ready")
        probs_turned, pT_dve, pT_act = sem("probs_turned"), sem("pT_dve"), sem("pT_act")
        pv_done, out_high, out_low = sem("pv_done"), sem("out_high"), sem("out_low")
        merged_ready = sem("merged_ready")
        x1_ready = sem("x1_ready")
        router_ps, top_ready = sem("router_ps"), sem("top_ready")
        mask_ready, rank_ps, wsel_ready = sem("mask_ready"), sem("rank_ps"), sem("wsel_ready")
        wT_ps, wT_ok = sem("wT_ps"), sem("wT_ok")
        routed = sem("routed")
        P_ready, gathered, XT_ready = sem("P_ready"), sem("gathered"), sem("XT_ready")
        PW_ready, WT_ps, WT_ready = sem("PW_ready"), sem("WT_ps"), sem("WT_ready")
        gate_ready, gu_drained, sig_ready = sem("gate_ready"), sem("gu_drained"), sem("sig_ready")
        prod_ready, act_ready = sem("prod_ready"), sem("act_ready")
        aT_ps, aT_ready, y_ready = sem("aT_ps"), sem("aT_ready"), sem("y_ready")
        sums_done = sem("sums_done")
        final_ready = sem("final_ready")
        dve_chain = sem("dve_chain")
        eps_ready = sem("eps_ready")

        block = ctx.enter_context(nc.Block())

        def front_landed(eng, i):
            eng.wait_ge(landed[i % FRONT_RING], 16 * (i // FRONT_RING + 1))

        def ring_slot(c):
            return (c + SCORE_SLOT) % RING

        def front_fills(r):
            return len(range(r, NF, FRONT_RING)) if r < FRONT_RING else 0

        def bcast(ap, axis, n):
            dims = [list(d) for d in ap.ap]
            return bass.AP(ap.tensor, ap.offset, dims[:axis] + [[0, n]] + dims[axis:])

        def reversed_tiles(ap):
            dims = [list(d) for d in ap.ap]
            step, n = dims[-1]
            return bass.AP(ap.tensor, ap.offset + (P - 1) * step, dims[:-1] + [[P * step, n // P], [-step, P]])

        def output_parts(o):
            b, n = output_blocks(o)
            src = ps[:, 4 + o % 2, 0:n * S]
            if UNITS[last_unit_of(o)][0] == "C":
                return qkP[:, b:b + 2, :], mkP[:, b - 20:b - 18, :], src.rearrange("p (h q) -> p h q", h=2)
            low = b + (4 if b < 4 else 2)
            return (qkP[:, b, :].rearrange("p (t q) -> p t q", t=T), qkP[:, low, :].rearrange("p (t q) -> p t q", t=T),
                    reversed_tiles(src))

        @block.sync
        def _(sp):
            def load_weights(e, j, r):
                if j < KC:
                    src = w_gu[bass.ds(e, 1), :, j, :].rearrange("o p c -> (o p) c")
                    dst = ring[:, r, :]
                else:
                    src = w_dn[bass.ds(e, 1), :, 2 * (j - KC):2 * (j - KC) + 2, :].rearrange("o p k c -> (o p) k c")
                    dst = ring[:, r, :].rearrange("p (k c) -> p k c", k=2)
                sp.dma_start(dst, src).then_inc(landed[r], 16)

            for tt in range(T):
                sp.dma_start(mem_raw[:, tt, :], t["mem"].rearrange("b (t p) d -> (b p) t d", p=P)[:, tt, :]).then_inc(mem_in[tt], 16)
            sp.dma_start(ident[:], t["ident"]).then_inc(first_in, 16)
            sp.dma_start(g_rows[:], t["g_rows"]).then_inc(first_in, 16)
            for i in range(NF):
                if i == 1:
                    sp.dma_start(x[:], t["x"].rearrange("b (t p) d -> (b p) t d", p=P)).then_inc(x_in, 16)
                    sp.dma_start(t5_in[0:T5_BUCKETS, :], t["t5_rel_bias"]).then_inc(t5_in_done, 16)
                    sp.dma_start(t5_in[T5_BUCKETS:T5_BUCKETS + 3, :], t["group_of_head"]).then_inc(t5_in_done, 16)
                    sp.dma_start(onehot[:], t["bucket_onehot"]).then_inc(t5_in_done, 16)
                if i >= FRONT_RING:
                    sp.wait_ge(chunk_used, i - FRONT_RING + 1)
                kind, n = FRONT[i]
                dst = ring[:, i % FRONT_RING, :]
                if kind in ("mem", "in", "out"):
                    src = {"mem": w_mem, "in": w_in, "out": w_out}[kind][:, :, n * SLOTS_W:(n + 1) * SLOTS_W]
                    dst = dst.rearrange("p (k c) -> p k c", k=KC)
                elif kind == "branch_b":
                    src, dst = w_br[kind], dst.rearrange("p (k c) -> p k c", k=2)
                else:
                    src, dst = w_br[kind][:, :, n * 512:(n + 1) * 512], dst.rearrange("p (k c) -> p k c", k=4)
                sp.dma_start(dst, src).then_inc(landed[i % FRONT_RING], 16)
                if i in EARLY_AFTER:
                    if i == min(EARLY_AFTER):
                        sp.wait_ge(pv_done, NU)
                        sp.wait_ge(chunk_used, LAST_A + 1)
                    for c in EARLY_AFTER[i]:
                        load_weights(0, c, ring_slot(c))
                if i == T5_STORE_AFTER:
                    sp.wait_ge(t5_copied, 1)
                    sp.dma_start(t5_scratch, t5_rows).then_inc(t5_saved, 16)
                    sp.wait_ge(t5_saved, 16)
                for u in range(2, NU):
                    if i != IMAGE_AFTER[u]:
                        continue
                    if u - 2 >= IMAGES:
                        sp.wait_ge(scores_drained, u - IMAGES + 1)
                    row = image_rows(u)
                    rows, row = (na_rows, row) if row < NA_HEADS else (t5_scratch, row - NA_HEADS)
                    sp.dma_start(image[:, (u - 2) % IMAGES], bass.AP(rows.tensor, row * REL, [[1, P], [REL, 2], [1, IMG]])
                                 ).then_inc(image_in[(u - 2) % IMAGES], 16)

            def load_bias(e, bias_slot):
                sp.dma_start(brow[64 * bias_slot:64 * bias_slot + 1, :], b_gu[0, bass.ds(e, 1), :]
                             ).then_inc(brow_in[bias_slot], 16)

            def load_expert(e, c, bias_slot, wait_for):
                for j in range(EXPERT_CHUNKS):
                    r = ring_slot(c + j)
                    wait_for(j)
                    if j == 0:
                        load_bias(e, bias_slot)
                    load_weights(e, j, r)

            def first_lap(n):
                def wait_for(j):
                    c = EXPERT_CHUNKS * n + j
                    r = ring_slot(c)
                    if j == 0 and n >= 2:
                        sp.wait_ge(chunk_used, NF + EXPERT_CHUNKS * (n - 2) + 1)
                    if c >= RING:
                        sp.wait_ge(chunk_used, NF + c - RING + 1)
                    elif r < FRONT_RING:
                        sp.wait_ge(chunk_used, max(i for i in range(NF) if i % FRONT_RING == r) + 1)
                    elif r < SCORE_SLOT:
                        sp.wait_ge(chunk_used, NF)
                return wait_for

            sp.wait_ge(merged_ready, 4)
            sp.dma_start(iota, bass.AP(t["iota"].tensor, 0, [[0, P], [1, D]])).then_inc(iota_in, 16)
            for j in range(EARLY, EXPERT_CHUNKS):
                if j == EXPERT_CHUNKS - 1:
                    sp.wait_ge(chunk_used, NF)
                    sp.dma_start(b_dn, t["expert_b_down"].rearrange("l e c -> (l e) c")).then_inc(b_dn_in, 16)
                    load_bias(0, 0)
                first_lap(0)(j)
                load_weights(0, j, ring_slot(j))
            sp.dma_start(final_g, bass.AP(t["final_norm_g"].tensor, 0, [[0, P], [1, D]])).then_inc(final_g_in, 16)
            for e in range(1, 4):
                load_expert(e, EXPERT_CHUNKS * e, e % 2, first_lap(e))
            with sp.Fori(1, EXPERTS // 4) as it:
                for q in range(4):
                    def wait_for(j):
                        sp.wait_ge(chunk_used, it * (4 * EXPERT_CHUNKS) + (NF + EXPERT_CHUNKS * q + j - RING + 1))
                    load_expert(it * 4 + q, EXPERT_CHUNKS * q, q % 2, wait_for)
            sp.wait_ge(routed, 1)
            n_over = sp.value_load(ovf[0:1, MAX_OVERFLOW:MAX_OVERFLOW + 1], min_val=0, max_val=MAX_OVERFLOW)
            with sp.If(0 < n_over):
                with sp.Fori(0, MAX_OVERFLOW) as b:
                    with sp.If(b < n_over):
                        e_b = sp.value_load(ovf[0:1, bass.ds(b, 1)], min_val=0, max_val=EXPERTS - 1)

                        def wait_for(j):
                            sp.wait_ge(chunk_used, b * EXPERT_CHUNKS + (NF + EXPERT_CHUNKS * (EXPERTS - 1) + j + 1))
                        load_expert(e_b, 0, 0, wait_for)
            for tt in range(T):
                sp.wait_ge(final_ready, 2 * tt + 2)
                sp.dma_start(t["out"].rearrange("b (t p) d -> (b p) t d", p=P)[:, tt, :], final[:, tt, :]).then_inc(out_saved, 16)
            sp.wait_ge(out_saved, 32)

        @block.gpsimd
        def _(pool):
            pool.wait_ge(mem_in[1], 16)
            pool.dma_start(na_mask[:], t["na_mask"]).then_inc(consts_in, 16)
            pool.dma_start(earlier[:], t["earlier"]).then_inc(consts_in, 16)
            pool.dma_start(stack4[:], t["stack4"]).then_inc(consts_in, 16)
            pool.dma_start(rw[:], t["router_w"].rearrange("l (k p) e -> (l p) k e", p=P)).then_inc(consts_in, 16)
            pool.dma_start(rb[:], bass.AP(t["router_b"].tensor, 0, [[0, P], [1, EXPERTS]])).then_inc(consts_in, 16)
            for i in range(NF):
                front_landed(pool, i)
                for h in range(2):
                    half = slice(h * CHUNK // 2, (h + 1) * CHUNK // 2)
                    pool.wait_ge(high_ready, 2 * i + h + 1)
                    last = nc.gpsimd.tensor_tensor(wHL[:, i % 2, 1, half], ring[:, i % FRONT_RING, half],
                                                   wHL[:, i % 2, 0, half].bitcast(F32), ALU.subtract)
                last.then_inc(low_ready, 1)
            pool.wait_ge(rstd_ready, 1)
            for tt in range(T):
                last = nc.gpsimd.tensor_scalar(xn[:, tt, :], x[:, tt, :], rstd[:, 2, tt:tt + 1], None, ALU.mult)
            last.then_inc(normed, 1)

        @block.tensor
        def _(pe):
            def mm(out, lhsT, rhs, start, stop, **kw):
                return nc.tensor.matmul(out, lhsT, rhs, start=start, stop=stop, **kw)

            def turn(src, m, first_bank):
                pe.wait_ge(normed, m + 1)
                for k in range(KC):
                    for tt in range(T):
                        last = nc.tensor.transpose(ps[:, first_bank + k // 2, (k % 2) * S + tt * P:(k % 2) * S + (tt + 1) * P],
                                                   src[:, tt, k * P:(k + 1) * P], ident[:])
                    if k % 2:
                        last.then_inc(turned, 1)

            pe.wait_ge(first_in, 32)
            nc.tensor.transpose(ps[:, 6, 0:3 * KC], g_rows[:], ident[0:3 * KC, 0:3 * KC]).then_inc(gcols_ps, 1)
            turn(mem_n, 0, 0)

            def head_scores(u):
                kind, j, g = UNITS[u]
                pe.wait_ge(front_evac, QK_DONE[kind])
                if u:
                    pe.wait_ge(scores_drained, u)
                else:
                    pe.wait_ge(h_low, 8)
                for tt in range(T):
                    for hh in range(2):
                        out = ps[:, 2 + hh, tt * S:(tt + 1) * S]
                        if kind == "C":
                            h = 2 * j + hh
                            last = mm(out, qkT[:, 20 + h, tt * P:(tt + 1) * P], mkT[:, h, :], True, True)
                        else:
                            qb, kb, _ = unit_blocks(u)
                            rows = slice(64 * hh, 64 * hh + 64)
                            last = mm(out, qkT[rows, qb, tt * P:(tt + 1) * P], qkT[rows, kb, :], True, True)
                last.then_inc(scores_ready, 1)

            def turn_probs(u):
                pe.wait_ge(probs_ready, u + 1)
                if u == 0:
                    pe.wait_ge(t5_copied, 1)
                else:
                    pe.wait_ge(pT_dve, u)
                    pe.wait_ge(pT_act, u)
                for hh in range(2):
                    for kt in range(T):
                        for tt in range(T):
                            last = nc.tensor.transpose(ps[:, 6 + hh, kt * S + tt * P:kt * S + (tt + 1) * P],
                                                       scores[:, u % 4, hh, tt, kt * P:(kt + 1) * P], ident[:])
                last.then_inc(probs_turned, 1)

            def attend(u):
                kind, j, g = UNITS[u]
                o = OUTPUT_OF[u]
                pe.wait_ge(pT_dve, u + 1)
                pe.wait_ge(pT_act, u + 1)
                pe.wait_ge(front_evac, QKV_DONE[kind])
                if o >= 2:
                    pe.wait_ge(out_low, o - 1)
                for kt in range(T):
                    for hh in range(2):
                        rhs = pT[:, u % 2, hh, kt, :]
                        if kind == "C":
                            continue
                        _, _, vc = unit_blocks(u)
                        last = mm(ps[64 * hh:64 * hh + 64, 4 + o % 2, 0:S], v[:, kt, vc + 64 * hh:vc + 64 * hh + 64], rhs,
                                  kt == 0 and g == 0, kt == T - 1 and (kind == "A" or g == 2))
                if kind == "C":
                    for hh in range(2):
                        for kt in range(T):
                            h = 2 * j + hh
                            last = mm(ps[:, 4 + o % 2, hh * S:(hh + 1) * S], mv[:, kt, h * P:(h + 1) * P],
                                      pT[:, u % 2, hh, kt, :], kt == 0, kt == T - 1)
                last.then_inc(pv_done, 1)

            def turn_x1(s):
                pe.wait_ge(front_evac, PLAIN[OUT0 + s + 1])
                for k in range(2):
                    for tt in range(T):
                        last = nc.tensor.transpose(ps[:, 2 + s, k * S + tt * P:k * S + (tt + 1) * P],
                                                   x[:, tt, (2 * s + k) * P:(2 * s + k + 1) * P], ident[:])
                last.then_inc(x1_turned, 1)

            def router_part(s):
                pe.wait_ge(x1T_dve if s % 2 else x1T_act, s // 2 + 1)
                for k in range(2):
                    last = mm(ps[32 * s:32 * s + EXPERTS, 6, 0:S], rw[:, 2 * s + k, :], x1T[:, 2 * s + k, :], k == 0, k == 1)
                return last

            def parts_of_chunk(i, a, k, kc):
                if a == 0 and k % (kc // 2) == 0:
                    pe.wait_ge(high_ready, 2 * i + 1 + k // (kc // 2))
                if a == 2 and k == 0:
                    pe.wait_ge(low_ready, i + 1)

            def turn_merged(q):
                pe.wait_ge(merged_ready, q + 1)
                for k in range(2):
                    for tt in range(T):
                        last = nc.tensor.transpose(ps[:, MERGE_BANK[q], k * S + tt * P:k * S + (tt + 1) * P],
                                                   xn[:, tt, (2 * q + k) * P:(2 * q + k + 1) * P], ident[:])
                last.then_inc(turned, 1)

            def products(i, h, weights_out, turn_no=None):
                w = wHL[:, i % 2].rearrange("p a (k c) -> p a k c", k=KC)
                order = [(a, k) for a in range(3) for k in range(KC)]
                if i == OUT0:
                    order.sort(key=lambda ak: (ak[0] == 2, ak[1] >= 6))
                for b in range(2):
                    for step, (a, k) in enumerate(order):
                        ha, wa = PART_PAIRS[a]
                        if i == OUT0 and b == 0 and (a, k) == (0, 6):
                            turn_merged(3)
                        if b == 0:
                            parts_of_chunk(i, a, k, KC)
                            if turn_no is not None and a < 2 and k % 2 == 0:
                                pe.wait_ge(h_low if a else h_high, 4 * turn_no + k // 2 + 1)
                        if weights_out:
                            lhsT, rhs = w[:, wa, k, b * P:(b + 1) * P], h[:, ha, k, :]
                        else:
                            lhsT, rhs = h[:, ha, k, b * P:(b + 1) * P], w[:, wa, k, :]
                        last = mm(ps[:, PLAIN[i] % 2, b * S:(b + 1) * S], lhsT, rhs, step == 0, step == len(order) - 1)
                last.then_inc(chunk_used, 1)

            for i, (kind, n) in enumerate(FRONT):
                if i == 0:
                    pe.wait_ge(h_low, 1)
                if i == 1:
                    pe.wait_ge(gcols_ok, 1)
                    turn(xn, 1, 4)
                if i == 4:
                    pe.wait_ge(h_low, 8)
                    pe.wait_ge(t5_in_done, 48)
                    mm(ps[0:DIL_HEADS, 7, :], t5_in[:], onehot[:], True, True).then_inc(t5_ps, 1)
                if kind.startswith("branch"):
                    pe.wait_ge(scores_drained, NU)
                    if i - PLAIN[i]:
                        pe.wait_ge(branch_evac, i - PLAIN[i])
                    pe.wait_ge(out_low, {"branch_a": 6, "branch_c": 2, "branch_b": 8}[kind])
                    outs = {"branch_a": (2, 3, 4, 5), "branch_c": (0, 1), "branch_b": (6, 7)}[kind]
                    high = [b + a for b, n_blocks in map(output_blocks, outs) for a in range(n_blocks)]
                    low = {"branch_a": [4 + b for b in high], "branch_b": [2 + b for b in high], "branch_c": [0, 1, 2, 3]}[kind]
                    lows = mkP if kind == "branch_c" else qkP
                    halves, kc = (2, 2) if kind == "branch_b" else (1, 4)
                    w = wHL[:, i % 2].rearrange("p a (k h c) -> p a k h c", k=kc, h=halves)
                    for half in range(halves):
                        for tt in range(T):
                            for a, (oa, wa) in enumerate(PART_PAIRS):
                                for k in range(kc):
                                    if half == 0 and tt == 0:
                                        parts_of_chunk(i, a, k, kc)
                                    lhsT = (lows[:, low[k]] if oa else qkP[:, high[k]])[:, tt * P:(tt + 1) * P]
                                    last = mm(ps[:, 2 + 2 * half + tt, :], lhsT, w[:, wa, k, half, :],
                                              k == 0 and a == 0, k == kc - 1 and a == 2)
                    last.then_inc(chunk_used, 1)
                else:
                    if i >= 2:
                        pe.wait_ge(front_evac, PLAIN[i] - 1)
                    products(i, {"mem": mHL, "in": hHL, "out": mergedHL}[kind], (kind == "mem" and n < 2) or (kind == "in" and n in QKT),
                             {0: 0, OUT0: 2}.get(i))
                if i > OUT0:
                    turn_x1(i - OUT0 - 1)
                if i in STEP_AFTER:
                    s = STEP_AFTER[i]
                    if s < NU:
                        head_scores(s)
                    if 0 <= s - TURN_LAG < NU:
                        turn_probs(s - TURN_LAG)
                    if 0 <= s - PV_LAG < NU:
                        attend(s - PV_LAG)
                if ONLY_B < i < OUT0:
                    turn_merged(i - ONLY_B - 1)

            turn_x1(3)
            pe.wait_ge(consts_in, 80)
            for c in range(4):
                last = router_part(c)
            last.then_inc(parts_ps, 1)
            pe.wait_ge(parts_in, 1)
            for tt in range(T):
                last = mm(ps[:, 7, 128 + tt * EXPERTS:128 + (tt + 1) * EXPERTS], router_parts[:, tt * P:(tt + 1) * P], stack4[:],
                          True, True)
            last.then_inc(router_ps, 1)
            pe.wait_ge(mask_ready, 1)
            mm(ps[:, 7, 0:EXPERTS], earlier[:], mask[:, 0, :], True, True)
            mm(ps[:, 7, 32:32 + EXPERTS], ones[:], mask[:, 0, :], True, False)
            mm(ps[:, 7, 32:32 + EXPERTS], earlier[:], mask[:, 1, :], False, True)
            mm(ps[:, 7, 64:64 + EXPERTS], ones[:], mask[:, 0, :], True, False)
            mm(ps[:, 7, 64:64 + EXPERTS], ones[:], mask[:, 1, :], False, True).then_inc(rank_ps, 1)
            def gather_half(half, width, bank=3):
                for k in range(4):
                    for tt in range(T):
                        last = mm(ps[:, bank, k * P:k * P + width], xn[:, tt, (4 * half + k) * P:(4 * half + k + 1) * P],
                                  P_pair[:, tt, 0:width], tt == 0, tt == T - 1)
                last.then_inc(gathered, 1)

            def scatter(by_bank=None):
                for tt in range(T):
                    for hn in range(2):
                        if by_bank and tt + hn:
                            last.then_inc(by_bank, 1)
                        last = mm(ps[:, 4 + 2 * tt + hn, :], WT_of[0][64 * hn:64 * hn + 64, tt * P:(tt + 1) * P],
                                  y_sb[64 * hn:64 * hn + 64, :], False, False, skip_group_check=True)
                if by_bank:
                    last.then_inc(by_bank, 1)

            WT_of = [None]

            def expert(n, c, fills, wt_slot, bias_slot, bias_fill, xt, xt_fill, gather, wait_rows=None):
                def slot(j):
                    return ring_slot(c + j)

                def chunk_landed(j):
                    pe.wait_ge(landed[slot(j)], (fills + ((c + j) // RING + 1 + front_fills(slot(j)))) * 16)

                pe.wait_ge(brow_in[bias_slot], bias_fill)
                pe.wait_ge(gu_drained, n + 1)
                for b in range(2):
                    for h in range(2):
                        mm(ps[64 * h:64 * h + 64, b, :], ones[64 * bias_slot:64 * bias_slot + 1, 0:BLK],
                           brow[64 * bias_slot:64 * bias_slot + 1, b * D + 512 * h:b * D + 512 * (h + 1)], True, False)
                if wait_rows:
                    wait_rows()
                for k in range(KC):
                    chunk_landed(k)
                    for b in range(2):
                        for h in range(2):
                            last = mm(ps[64 * h:64 * h + 64, b, :], xt[:, k, :],
                                      ring[:, slot(k), b * D + 512 * h:b * D + 512 * (h + 1)], False, k == KC - 1)
                    last.then_inc(chunk_used, 1)
                    if k == 3:
                        if WT_of[0] is None:
                            open_sums()
                        else:
                            pe.wait_ge(y_ready, n)
                            scatter()
                        WT_of[0] = WT[:, wt_slot, :]
                        pe.wait_ge(PW_ready, n + 1)
                        for tt in range(T):
                            last = nc.tensor.transpose(ps[:, 3, tt * P:(tt + 1) * P], PW[:, tt, :], ident[:])
                        last.then_inc(WT_ps, 1)
                gather()
                pe.wait_ge(act_ready, n + 1)
                for f in range(4):
                    last = nc.tensor.transpose(ps[:, 2, f * P:(f + 1) * P], sig[:, f * P:(f + 1) * P], ident[:])
                last.then_inc(aT_ps, 1)
                pe.wait_ge(aT_ready, n + 1)
                pe.wait_ge(XT_ready, xt_fill)
                for j in range(KC, EXPERT_CHUNKS):
                    chunk_landed(j)
                    for kk in range(2):
                        k = 2 * (j - KC) + kk
                        for hn in range(2):
                            last = mm(ps[64 * hn:64 * hn + 64, 3, :], aT[:, k % 4, BLK * (k // 4):BLK * (k // 4) + BLK],
                                      ring[:, slot(j), kk * D + 512 * hn:kk * D + 512 * (hn + 1)],
                                      k == 0, k == KC - 1)
                    last.then_inc(chunk_used, 1)

            pe.wait_ge(wsel_ready, 1)
            for tt in range(T):
                nc.tensor.transpose(ps[0:EXPERTS, 1, tt * P:(tt + 1) * P], w_sel[:, tt, :], ident[:]
                                    ).then_inc(wT_ps if tt else WT_ps, 1)
            def open_sums():
                pe.wait_ge(wT_ok, 1)
                pe.wait_ge(b_dn_in, 16)
                for tt in range(T):
                    for hn in range(2):
                        mm(ps[:, 4 + 2 * tt + hn, :], wT_sel[:, tt * P:(tt + 1) * P], b_dn[:, 512 * hn:512 * (hn + 1)],
                           True, False, skip_group_check=True)

            pe.wait_ge(P_ready, 1)
            pe.wait_ge(normed, 3)
            gather_half(0, 2 * BLK)
            gather_half(1, 2 * BLK, 2)
            def four_experts(it):
                for q in range(4):
                    n = it * 4 + q

                    def gather():
                        pe.wait_ge(P_ready, it * 2 + (q // 2 + 2))
                        pe.wait_ge(WT_ready, n + 1)
                        gather_half(q % 2, 2 * BLK)

                    def wait_rows():
                        pe.wait_ge(XT_ready, n + 2)

                    expert(n, EXPERT_CHUNKS * q, it * 3, q % 2, q % 2, (it * 2 + (q // 2 + 1)) * 16,
                           XT[:, q // 2, :, BLK * (q % 2):BLK * (q % 2) + BLK], n + 3, gather,
                           None if q % 2 else wait_rows)
            four_experts(0)
            with pe.Fori(1, EXPERTS // 4) as it:
                four_experts(it)
            n_over = pe.value_load(ovf[0:1, MAX_OVERFLOW:MAX_OVERFLOW + 1], min_val=0, max_val=MAX_OVERFLOW)
            with pe.If(0 < n_over):
                with pe.Fori(0, MAX_OVERFLOW) as b:
                    with pe.If(b < n_over):
                        n = b + EXPERTS
                        pe.wait_ge(P_ready, b + (EXPERTS // 2 + 2))
                        pe.wait_ge(y_ready, n)
                        for half in range(2):
                            pe.wait_ge(XT_ready, b * 2 + (EXPERTS + 2 + half))
                            gather_half(half, BLK)
                        pe.wait_ge(XT_ready, b * 2 + (EXPERTS + 4))
                        WT_of[0] = WT[:, 1, :]
                        expert(n, 0, b + EXPERTS * EXPERT_CHUNKS // RING, 1, 0, (b + (EXPERTS // 2 + 1)) * 16, XT[:, 0, :, 0:BLK], b * 2 + (EXPERTS + 4),
                               lambda: pe.wait_ge(WT_ready, n + 1))
            pe.wait_ge(y_ready, EXPERTS)
            with pe.If(0 < n_over):
                pe.wait_ge(y_ready, n_over + EXPERTS)
            WT_of[0] = WT[:, 1, :]
            scatter(sums_done)

        @block.scalar
        def _(act):
            def square_sums(src, junk, m, arrive=None):
                for tt in range(T):
                    if arrive:
                        act.wait_ge(arrive[tt], 16)
                    last = nc.scalar.activation(junk[:, tt, :], src[:, tt, :], ACT.Square, accum_out=sumsq[:, m, tt:tt + 1])
                last.then_inc(sq_done, 1)
                act.wait_ge(sq_done, m + 1)
                nc.scalar.activation(rstd[:, m, :], sumsq[:, m, :], ACT.Sqrt, scale=1.0 / D, bias=eps[:, 0:1]
                                     ).then_inc(std_ready, 1)

            def high_of_turned(parts, turn_no, gain, banks, first=0):
                for q, bank in enumerate(banks, first):
                    act.wait_ge(turned, 4 * turn_no + q + 1)
                    if gain is None:
                        last = nc.scalar.copy(parts[:, 0, 2 * q:2 * q + 2, :], ps[:, bank, :].rearrange("p (k t) -> p k t", k=2))
                    else:
                        for k in (2 * q, 2 * q + 1):
                            last = nc.scalar.mul(parts[:, 0, k, :], ps[:, bank, (k % 2) * S:(k % 2 + 1) * S],
                                                 g_cols[:, gain * KC + k:gain * KC + k + 1])
                    last.then_inc(h_high, 1)

            def high_part(i):
                front_landed(act, i)
                if i >= 2:
                    act.wait_ge(chunk_used, i - 1)
                for h in range(2):
                    half = slice(h * CHUNK // 2, (h + 1) * CHUNK // 2)
                    nc.scalar.copy(wHL[:, i % 2, 0, half], ring[:, i % FRONT_RING, half]).then_inc(high_ready, 1)

            act.wait_ge(eps_ready, 1)
            nc.scalar.activation(sumsq[:, 3, 0:1], eps[:], ACT.Sqrt)
            square_sums(mem_raw, mem_n, 0, arrive=mem_in)
            act.wait_ge(gcols_ok, 1)
            high_of_turned(mHL, 0, 0, range(4))
            act.wait_ge(x_in, 16)
            square_sums(x, xn, 1)
            act.wait_ge(high_ready, 2)
            high_part(1)

            def exps(u):
                kind, j, g = UNITS[u]
                o = OUTPUT_OF[u]
                act.wait_ge(max_ready, o + 1)
                for hh in range(2):
                    for tt in range(T):
                        p = scores[:, u % 4, hh, tt, :]
                        last = nc.scalar.activation(p, p, ACT.Exp, bias=neg_max[:, o, 2 * hh + tt:2 * hh + tt + 1],
                                                    accum_out=exp_sum[:, u, 2 * hh + tt:2 * hh + tt + 1])
                last.then_inc(exp_done, 1)

            for i, (kind, n) in enumerate(FRONT):
                if i == 1:
                    high_of_turned(hHL, 1, 1, range(4, 8))
                if i + 2 < NF:
                    high_part(i + 2)
                if kind in ("mem", "in"):
                    act.wait_ge(chunk_used, i + 1)
                    if kind == "in" and n in GATE_BRANCH:
                        act.wait_ge(t5_saved, 16)
                        if n < 25 and i > LAST_A:
                            act.wait_ge(branch_evac, 2)
                    src = ps[:, PLAIN[i] % 2, :].rearrange("p (t c) -> p t c", t=2)
                    if kind == "mem":
                        if n < 2:
                            e = nc.scalar.copy(mkT[:, 2 * n:2 * n + 2, :], src)
                        else:
                            e = nc.scalar.copy(mv[:, :, (n - 2) * 256:(n - 1) * 256], src)
                    elif n in Q_SCALE and n < 15:
                        e = nc.scalar.mul(qkT[:, QKT[n]:QKT[n] + 2, :].rearrange("p b (t q) -> p b t q", t=T),
                                          reversed_tiles(src), Q_SCALE[n])
                    elif n in QKT:
                        e = nc.scalar.mul(qkT[:, QKT[n]:QKT[n] + 2, :], src, Q_SCALE.get(n, 1.0))
                    elif n in V_COL:
                        e = nc.scalar.copy(v[:, :, V_COL[n]:V_COL[n] + 256], src)
                    else:
                        buf, c = GATE_BRANCH[n]
                        e = nc.scalar.activation(gates[:, buf, :, c * 256:(c + 1) * 256], src, ACT.Sigmoid)
                    e.then_inc(front_evac, 1)
                if ONLY_B < i < OUT0:
                    q = i - ONLY_B - 1
                    high_of_turned(mergedHL, 2, None, MERGE_BANK[q:q + 1], q)
                    if i == OUT0 - 1:
                        high_of_turned(mergedHL, 2, None, MERGE_BANK[3:], 3)
                        nc.scalar.activation(sumsq[:, 3, 0:1], eps[:], ACT.Sqrt)
                if i in STEP_AFTER:
                    s = STEP_AFTER[i]
                    u = s - TURN_LAG
                    if 0 <= u < NU:
                        act.wait_ge(probs_turned, u + 1)
                        if u >= 2:
                            act.wait_ge(pv_done, u - 1)
                        nc.scalar.copy(pT[:, u % 2, 1], ps[:, 7, :].rearrange("p (k q) -> p k q", k=2)).then_inc(pT_act, 1)
                    if s < NU and s == last_unit_of(OUTPUT_OF[s]):
                        for w in range(NU):
                            if OUTPUT_OF[w] == OUTPUT_OF[s]:
                                exps(w)
                    u = s - PV_LAG
                    if 0 <= u < NU and u == last_unit_of(OUTPUT_OF[u]):
                        o = OUTPUT_OF[u]
                        act.wait_ge(pv_done, u + 1)
                        high, _, src = output_parts(o)
                        nc.scalar.copy(high, src).then_inc(out_high, 1)
            for c in range(4):
                act.wait_ge(front_evac, PLAIN[OUT0 + c + 1])
                if c:
                    act.wait_ge(square_parts, c)
                for tt in range(T):
                    last = nc.scalar.activation(sq_tmp[:, tt, :], x[:, tt, c * SLOTS_W:(c + 1) * SLOTS_W], ACT.Square,
                                                accum_out=part_sums[:, tt, c:c + 1])
                last.then_inc(square_parts, 1)
                if c % 2 == 0:
                    act.wait_ge(x1_turned, c + 1)
                    for k in (2 * c, 2 * c + 1):
                        last = nc.scalar.mul(x1T[:, k, :], ps[:, 2 + c, (k % 2) * S:(k % 2 + 1) * S],
                                             g_cols[:, 2 * KC + k:2 * KC + k + 1])
                    last.then_inc(x1T_act, 1)
            act.wait_ge(sums_ready, 1)
            nc.scalar.activation(rstd[:, 2, :], sumsq[:, 2, :], ACT.Sqrt, scale=1.0 / D, bias=eps[:, 0:1]).then_inc(std_ready, 1)
            act.wait_ge(top_ready, 1)
            for tt in range(T):
                last = nc.scalar.activation(prob[:, tt, :], logits[:, tt, 0:EXPERTS], ACT.Exp, bias=neg_top[:, tt:tt + 1])
            last.then_inc(probs_exp, 1)

            def move_gathered(half, xt, width, count_before, bank=3):
                act.wait_ge(gathered, count_before + 1)
                for k in range(4):
                    c = 4 * half + k
                    last = nc.scalar.mul(xt[:, c, 0:width], ps[:, bank, k * P:k * P + width],
                                         g_cols[:, 2 * KC + c:2 * KC + c + 1])
                last.then_inc(XT_ready, 1)

            for half in range(2):
                move_gathered(half, XT[:, 0], 2 * BLK, half, 3 - half)

            def expert(n, wt_slot, gathered_next):
                act.wait_ge(WT_ps, n + 2)
                nc.scalar.copy(WT[:, wt_slot, :], ps[:, 3, 0:S]).then_inc(WT_ready, 1)
                act.wait_ge(gate_ready, n + 1)
                nc.scalar.activation(sig, gate_c, ACT.Sigmoid, scale=ALPHA).then_inc(sig_ready, 1)
                gathered_next()
                act.wait_ge(chunk_used, NF + EXPERT_CHUNKS * (n + 1))
                nc.scalar.copy(y_sb, ps[:, 3, :]).then_inc(y_ready, 1)

            with act.Fori(0, EXPERTS // 4) as it:
                for q in range(4):
                    n = it * 4 + q
                    expert(n, q % 2, lambda: move_gathered(q % 2, XT[:, (q // 2 + 1) % 2], 2 * BLK, n + 2))
            n_over = act.value_load(ovf[0:1, MAX_OVERFLOW:MAX_OVERFLOW + 1], min_val=0, max_val=MAX_OVERFLOW)
            with act.If(0 < n_over):
                with act.Fori(0, MAX_OVERFLOW) as b:
                    with act.If(b < n_over):
                        for half in range(2):
                            move_gathered(half, XT[:, 0], BLK, b * 2 + (EXPERTS + 2 + half))
                        expert(b + EXPERTS, 1, lambda: None)
            nc.scalar.activation(b_tmp[:, 0, 0:1], eps[:], ACT.Sqrt)
            for tt in range(T):
                for h in range(2):
                    cols = slice(512 * h, 512 * h + 512)
                    act.wait_ge(x1_ready, 2 * tt + h + 1)
                    last = nc.scalar.activation(final[:, tt, cols], x[:, tt, cols], ACT.Square,
                                                accum_out=part_sums[:, tt, h:h + 1])
                last.then_inc(sq_done, 1)
                act.wait_ge(sq_done, 2 + 2 * tt + 1)
                nc.scalar.activation(sumsq[:, 3, tt:tt + 1], part_sums[:, tt, 0:1], ACT.Identity, scale=1.0 / D,
                                     bias=eps[:, 0:1]).then_inc(sq_done, 1)
                act.wait_ge(sq_done, 2 + 2 * tt + 2)
                nc.scalar.activation(rstd[:, 3, tt:tt + 1], part_sums[:, tt, 1:2], ACT.Sqrt, scale=1.0 / D,
                                     bias=sumsq[:, 3, tt:tt + 1]).then_inc(std_ready, 1)

        @block.vector
        def _(dve):
            vec = nc.vector
            links = [0]

            def link(i):
                links[0] += 1
                i.then_inc(dve_chain, 1)
                dve.wait_ge(dve_chain, links[0])

            def normalise(src, dst, m):
                dve.wait_ge(std_ready, m + 1)
                link(vec.reciprocal(rstd[:, m, :], rstd[:, m, :]))
                for tt in range(T):
                    last = vec.tensor_scalar(dst[:, tt, :], src[:, tt, :], rstd[:, m, tt:tt + 1], None, ALU.mult)
                last.then_inc(normed, 1)

            def low_of_turned(parts, turn_no, gain, banks, first=0):
                for q, bank in enumerate(banks, first):
                    dve.wait_ge(h_high, 4 * turn_no + q + 1)
                    high = parts[:, 0, 2 * q:2 * q + 2, :].bitcast(F32)
                    src = ps[:, bank, :].rearrange("p (k t) -> p k t", k=2)
                    if gain is None:
                        last = vec.tensor_tensor(parts[:, 1, 2 * q:2 * q + 2, :], src, high, ALU.subtract)
                    else:
                        for k in range(2):
                            c = gain * KC + 2 * q + k
                            last = vec.scalar_tensor_tensor(parts[:, 1, 2 * q + k, :], src[:, k, :], g_cols[:, c:c + 1],
                                                            high[:, k, :], ALU.mult, ALU.subtract)
                    last.then_inc(h_low, 1)

            def merge(y, gate_buf, lo, width, add):
                m, g = xn[:, :, lo:lo + width], gates[:, gate_buf, :, lo:lo + width]
                if not add:
                    return vec.tensor_tensor(m, g, y, ALU.mult)
                link(vec.tensor_tensor(g, g, y, ALU.mult))
                return vec.tensor_tensor(m, m, g, ALU.add)

            vec.memset(eps[:], EPS).then_inc(eps_ready, 1)
            link(vec.memset(ones[:], 1.0))
            dve.wait_ge(gcols_ps, 1)
            vec.tensor_copy(g_cols[:, 0:3 * KC], ps[:, 6, 0:3 * KC]).then_inc(gcols_ok, 1)
            normalise(mem_raw, mem_n, 0)
            front_landed(dve, 0)
            for h in range(2):
                half = slice(h * CHUNK // 2, (h + 1) * CHUNK // 2)
                vec.tensor_copy(wHL[:, 0, 0, half], ring[:, 0, half]).then_inc(high_ready, 1)
            dve.wait_ge(gcols_ok, 1)
            low_of_turned(mHL, 0, 0, range(4))
            normalise(x, xn, 1)
            low_of_turned(hHL, 1, 1, range(4, 8))
            dve.wait_ge(t5_ps, 1)
            vec.tensor_copy(t5_rows, ps[0:DIL_HEADS, 7, :]).then_inc(t5_copied, 1)

            for i, (kind, n) in enumerate(FRONT):
                if kind in ("branch_a", "branch_c"):
                    dve.wait_ge(chunk_used, i + 1)
                    dve.wait_ge(front_evac, PLAIN[i])
                    merge(ps[:, 2:4, :], int(kind == "branch_c"), 512 * n, 512, kind == "branch_c").then_inc(branch_evac, 1)
                if ONLY_B <= i < OUT0:
                    q = i - ONLY_B
                    dve.wait_ge(chunk_used, ONLY_B + 1)
                    dve.wait_ge(front_evac, PLAIN[i + 1])
                    b = 2 + 2 * (q // 2)
                    merge(ps[:, b:b + 2, (q % 2) * SLOTS_W:(q % 2 + 1) * SLOTS_W], 0, q * SLOTS_W, SLOTS_W, True
                          ).then_inc(merged_ready, 1)
                    if q:
                        low_of_turned(mergedHL, 2, None, MERGE_BANK[q - 1:q], q - 1)
                    if q == 3:
                        low_of_turned(mergedHL, 2, None, MERGE_BANK[3:], 3)
                if kind == "out":
                    dve.wait_ge(chunk_used, i + 1)
                    xs = x[:, :, n * SLOTS_W:(n + 1) * SLOTS_W]
                    vec.tensor_tensor(xs, xs, ps[:, PLAIN[i] % 2, :].rearrange("p (t c) -> p t c", t=2), ALU.add
                                      ).then_inc(front_evac, 1)
                    if n in (1, 3):
                        dve.wait_ge(x1_turned, n + 1)
                        for k in (2 * n, 2 * n + 1):
                            last = vec.tensor_scalar(x1T[:, k, :], ps[:, 2 + n, (k % 2) * S:(k % 2 + 1) * S],
                                                     g_cols[:, 2 * KC + k:2 * KC + k + 1], None, ALU.mult)
                        last.then_inc(x1T_dve, 1)
                    if n == 3:
                        dve.wait_ge(square_parts, 4)
                        vec.tensor_reduce(sumsq[:, 2, :], part_sums, AX_X, ALU.add).then_inc(sums_ready, 1)
                if i in STEP_AFTER:
                    s = STEP_AFTER[i]
                    if s < NU:
                        kind_u, j, g = UNITS[s]
                        dve.wait_ge(scores_ready, s + 1)
                        if s >= 4:
                            dve.wait_ge(probs_turned, s - 3)
                        if kind_u != "C":
                            b = (s - 2) % IMAGES
                            dve.wait_ge(image_in[b], 16 * ((s - 2) // IMAGES + 1))
                            if kind_u == "A":
                                dve.wait_ge(consts_in, 80)
                                im = image[:, b].rearrange("p h (r c) -> p (h r) c", c=GRID_W)
                                link(vec.tensor_tensor(im, im, bcast(na_mask[:], 1, 2 * IMG // GRID_W), ALU.add))
                        for tt in range(T):
                            src = ps[:, 2:4, tt * S:(tt + 1) * S]
                            dst = scores[:, s % 4, :, tt, :]
                            if kind_u == "C":
                                last = vec.tensor_copy(dst, src)
                            else:
                                last = vec.tensor_tensor(dst, src, image[:, b, :, P - P * tt:P - P * tt + S], ALU.add)
                        last.then_inc(scores_drained, 1)
                        dve.wait_ge(scores_drained, s + 1)
                        link(vec.tensor_reduce(row_max[:, s, :], scores[:, s % 4].rearrange("p h t k -> p (h t) k"),
                                               AX_X, ALU.max))
                        o = OUTPUT_OF[s]
                        if s == last_unit_of(o):
                            if kind_u == "B":
                                link(vec.tensor_tensor(b_tmp[:, 0, :], row_max[:, s - 2, :], row_max[:, s - 1, :], ALU.max))
                                link(vec.tensor_tensor(row_max[:, s, :], b_tmp[:, 0, :], row_max[:, s, :], ALU.max))
                            vec.tensor_scalar(neg_max[:, o, :], row_max[:, s, :], -1.0, None, ALU.mult).then_inc(max_ready, 1)
                    u = s - TURN_LAG
                    if 0 <= u < NU:
                        dve.wait_ge(probs_turned, u + 1)
                        if u >= 2:
                            dve.wait_ge(pv_done, u - 1)
                        vec.tensor_copy(pT[:, u % 2, 0], ps[:, 6, :].rearrange("p (k q) -> p k q", k=2)).then_inc(pT_dve, 1)
                    if s < NU and s == last_unit_of(OUTPUT_OF[s]):
                        o = OUTPUT_OF[s]
                        dve.wait_ge(exp_done, s + 1)
                        total = exp_sum[:, s, :]
                        if UNITS[s][0] == "B":
                            link(vec.tensor_tensor(b_tmp[:, 0, :], exp_sum[:, s - 2, :], exp_sum[:, s - 1, :], ALU.add))
                            link(vec.tensor_tensor(b_tmp[:, 1, :], b_tmp[:, 0, :], exp_sum[:, s, :], ALU.add))
                            total = b_tmp[:, 1, :]
                        link(vec.reciprocal(inv_sum[:, o, :], total))
                        for w in range(NU):
                            if OUTPUT_OF[w] == o:
                                p = scores[:, w % 4].rearrange("p h t k -> p (h t) k")
                                vec.tensor_tensor(p, p, bcast(inv_sum[:, o, :], 2, S), ALU.mult).then_inc(probs_ready, 1)
                    u = s - PV_LAG
                    if 0 <= u < NU and u == last_unit_of(OUTPUT_OF[u]):
                        dve.wait_ge(out_high, OUTPUT_OF[u] + 1)
                        high, low, src = output_parts(OUTPUT_OF[u])
                        vec.tensor_tensor(low, src, high.bitcast(F32), ALU.subtract).then_inc(out_low, 1)
            link(vec.memset(logits[:, :, EXPERTS:], SENTINEL))
            link(vec.memset(keys[:, :, EXPERTS:], -NO_SLOT))
            vec.memset(b_tmp[:], 0.0).then_inc(gu_drained, 1)
            dve.wait_ge(std_ready, 3)
            vec.reciprocal(rstd[:, 2, :], rstd[:, 2, :]).then_inc(rstd_ready, 1)
            dve.wait_ge(parts_ps, 1)
            vec.tensor_copy(router_parts, ps[:, 6, 0:S]).then_inc(parts_in, 1)
            dve.wait_ge(rstd_ready, 1)
            dve.wait_ge(router_ps, 1)
            for tt in range(T):
                link(vec.scalar_tensor_tensor(logits[:, tt, 0:EXPERTS], ps[:, 7, 128 + tt * EXPERTS:128 + (tt + 1) * EXPERTS],
                                              rstd[:, 2, tt:tt + 1], rb[:], ALU.mult, ALU.add))
            for tt in range(T):
                link(vec.max(top8[:, tt, :], logits[:, tt, :]))
            vec.tensor_scalar(neg_top, top8[:, :, 0], -1.0, None, ALU.mult).then_inc(top_ready, 1)
            link(vec.memset(top8[:, :, TOP_K:], SENTINEL))
            for tt in range(T):
                link(vec.match_replace(replaced[:, tt, :], top8[:, tt, :], logits[:, tt, :], REPLACED))
            vec.tensor_tensor(mask, replaced[:, :, 0:EXPERTS], logits[:, :, 0:EXPERTS], ALU.not_equal).then_inc(mask_ready, 1)
            dve.wait_ge(mask_ready, 1)
            dve.wait_ge(probs_exp, 1)
            link(vec.tensor_tensor(prob_m, prob, mask, ALU.mult))
            link(vec.tensor_reduce(w_sum, prob_m, AX_X, ALU.add))
            link(vec.reciprocal(w_inv, w_sum))
            vec.tensor_tensor(w_sel, prob_m, bcast(w_inv, 2, EXPERTS), ALU.mult).then_inc(wsel_ready, 1)
            dve.wait_ge(rank_ps, 1)
            link(vec.tensor_scalar(tmp_a, mask, NO_SLOT, -NO_SLOT, ALU.mult, ALU.add))
            link(vec.tensor_tensor(keys[:, :, 0:EXPERTS], tmp_a, ps[:, 7, 0:T * EXPERTS].rearrange("p (t e) -> p t e", t=T),
                                   ALU.add))
            link(vec.tensor_copy(count, ps[:, 7, 64:64 + EXPERTS]))
            dve.wait_ge(wT_ps, 1)
            vec.tensor_copy(wT_sel, ps[0:EXPERTS, 1, 0:S]).then_inc(wT_ok, 1)

            def gather_matrix(col, width, slots):
                for tt in range(T):
                    last = vec.tensor_scalar(P_pair[:, tt, col:col + width], slots, keys_at[0][:, tt, keys_at[1]], None,
                                             ALU.is_equal)
                return last

            keys_at = [keys, slice(0, 1)]
            dve.wait_ge(iota_in, 16)
            gather_matrix(0, BLK, iota[:, 0:BLK])
            keys_at[1] = slice(1, 2)
            gather_matrix(BLK, BLK, iota[:, 0:BLK]).then_inc(P_ready, 1)
            link(vec.tensor_scalar(extra, count, float(BLK), None, ALU.is_gt))
            for lim in (2 * BLK, 3 * BLK):
                link(vec.tensor_scalar(tmp_a[:, 0, :], count, float(lim), None, ALU.is_gt))
                link(vec.tensor_tensor(extra, extra, tmp_a[:, 0, :], ALU.add))
            link(vec.tensor_tensor_scan(ends, extra, extra, 0.0, ALU.add, ALU.bypass))
            link(vec.tensor_tensor(tmp_a[:, 0, :], ends, extra, ALU.subtract))
            link(vec.tensor_scalar(tmp_a[:, 0, :], tmp_a[:, 0, :], float(BLK), NO_SLOT - BLK, ALU.mult, ALU.add))
            link(vec.tensor_tensor(okeys, keys[:, :, 0:EXPERTS], bcast(tmp_a[:, 0, :], 1, T), ALU.add))
            link(vec.tensor_scalar(tmp_b, keys[:, :, 0:EXPERTS], float(BLK), None, ALU.is_ge))
            link(vec.tensor_tensor(okeys, okeys, tmp_b, ALU.mult))
            link(vec.tensor_scalar(okeys, okeys, NO_SLOT, None, ALU.subtract))
            link(vec.tensor_tensor(ends_le, bcast(ends, 1, MAX_OVERFLOW), bcast(iota[:, 0:MAX_OVERFLOW], 2, EXPERTS), ALU.is_le))
            link(vec.tensor_reduce(ovf_f, ends_le, AX_X, ALU.add))
            link(vec.tensor_scalar(ovf_f, ovf_f, float(EXPERTS - 1), None, ALU.min))
            link(vec.tensor_copy(ovf[:, 0:MAX_OVERFLOW], ovf_f))
            vec.tensor_copy(ovf[:, MAX_OVERFLOW:], ends[:, EXPERTS - 1:EXPERTS]).then_inc(routed, 1)

            def expert(n, key_tile, slots, e):
                dve.wait_ge(WT_ps, n + 1)
                for tt in range(T):
                    last = vec.tensor_scalar(PW[:, tt, :].rearrange("p (a s) -> p a s", a=2), bcast(slots, 1, 2),
                                             key_tile[:, tt, e], w_sel[:, tt, e], ALU.is_equal, ALU.mult)
                last.then_inc(PW_ready, 1)
                dve.wait_ge(chunk_used, NF + EXPERT_CHUNKS * n + KC)
                vec.tensor_scalar(gate_c, ps[:, 0, :], LIMIT, None, ALU.min).then_inc(gate_ready, 1)
                vec.tensor_scalar(up_c, ps[:, 1, :], -LIMIT, LIMIT, ALU.max, ALU.min).then_inc(gu_drained, 1)
                dve.wait_ge(gate_ready, n + 1)
                dve.wait_ge(gu_drained, n + 2)
                vec.scalar_tensor_tensor(up_c, up_c, 1.0, gate_c, ALU.add, ALU.mult).then_inc(prod_ready, 1)
                dve.wait_ge(prod_ready, n + 1)
                dve.wait_ge(sig_ready, n + 1)
                vec.tensor_tensor(sig, up_c, sig, ALU.mult).then_inc(act_ready, 1)
                dve.wait_ge(aT_ps, n + 1)
                vec.tensor_copy(aT, ps[:, 2, :].rearrange("p (f s) -> p f s", f=4)).then_inc(aT_ready, 1)

            with dve.Fori(0, EXPERTS // 4) as it:
                for q in range(4):
                    n = it * 4 + q
                    if q % 2 == 0:
                        dve.wait_ge(gathered, n + 2)
                        for a in range(2):
                            keys_at[1] = bass.ds(n + (2 + a), 1)
                            last = gather_matrix(BLK * a, BLK, iota[:, 0:BLK])
                        last.then_inc(P_ready, 1)
                    expert(n, keys, iota[:, 0:BLK], bass.ds(n, 1))
            dve.wait_ge(routed, 1)
            n_over = dve.value_load(ovf[0:1, MAX_OVERFLOW:MAX_OVERFLOW + 1], min_val=0, max_val=MAX_OVERFLOW)
            with dve.If(0 < n_over):
                with dve.Fori(0, MAX_OVERFLOW) as b:
                    with dve.If(b < n_over):
                        e_b = dve.value_load(ovf[0:1, bass.ds(b, 1)], min_val=0, max_val=EXPERTS - 1)
                        slots = iota[:, bass.ds(b * BLK, BLK)]
                        dve.wait_ge(gathered, b * 2 + (EXPERTS + 2))
                        keys_at[0], keys_at[1] = okeys, bass.ds(e_b, 1)
                        gather_matrix(0, BLK, slots).then_inc(P_ready, 1)
                        expert(b + EXPERTS, okeys, slots, bass.ds(e_b, 1))
            for b in range(2 * T):
                tt, cols = b // 2, slice(512 * (b % 2), 512 * (b % 2) + 512)
                dve.wait_ge(sums_done, b + 1)
                vec.tensor_tensor(x[:, tt, cols], x[:, tt, cols], ps[:, 4 + b, :], ALU.add).then_inc(x1_ready, 1)
            dve.wait_ge(final_g_in, 16)
            dve.wait_ge(x1_ready, 2 * T)
            for tt in range(T):
                dve.wait_ge(std_ready, 3 + tt + 1)
                link(vec.reciprocal(rstd[:, 3, tt:tt + 1], rstd[:, 3, tt:tt + 1]))
                for cols in (slice(0, 512), slice(512, D)):
                    vec.scalar_tensor_tensor(final[:, tt, cols], x[:, tt, cols], rstd[:, 3, tt:tt + 1], final_g[:, cols],
                                             ALU.mult, ALU.mult).then_inc(final_ready, 1)


def t5_bucket(rel):
    half = T5_BUCKETS // 2
    exact = half // 2
    n = np.abs(rel)
    large = exact + (np.log(np.maximum(n, 1).astype(np.float32) / exact) / math.log(T5_MAX_DIST / exact)
                     * (half - exact)).astype(np.int32)
    return np.where(rel > 0, half, 0) + np.where(n < exact, n, np.minimum(large, half - 1))


def constants():
    rel = np.arange(REL) - (S - 1)
    onehot = np.zeros((T5_BUCKETS + 3, REL), np.float32)
    onehot[t5_bucket(rel), np.arange(REL)] = 1.0
    for g, (dil, window) in enumerate(zip(DIL, DIL_WINDOW)):
        ok = (rel % dil == 0) & (np.abs(rel) // dil <= window // 2 // dil)
        onehot[T5_BUCKETS + g] = np.where(ok, 0.0, NEG)
    group = np.zeros((3, DIL_HEADS), np.float32)
    for g in range(3):
        group[g, g * GROUP_HEADS:(g + 1) * GROUP_HEADS] = 1.0
    col = np.arange(GRID_W)
    start = np.clip(col - WIN_COLS // 2, 0, GRID_W - WIN_COLS)
    ok = (col[None] >= start[:, None]) & (col[None] < start[:, None] + WIN_COLS)
    na_mask = np.tile(np.where(ok, 0.0, NEG).astype(np.float32), (P // GRID_W, 1))[::-1].copy()
    return {"bucket_onehot": onehot, "group_of_head": group, "na_mask": na_mask, "ident": np.eye(P, dtype=np.float32),
            "stack4": np.tile(np.eye(EXPERTS, dtype=np.float32), (4, 1)),
            "earlier": np.triu(np.ones((P, P), np.float32), 1), "iota": np.arange(D, dtype=np.float32)}


_DIRECT = ["x", "mem", "w_in", "w_mem_kv", "t5_rel_bias", "w_branch_a", "w_branch_b", "w_branch_c", "w_out", "router_w",
           "router_b", "expert_w_gate_up", "expert_b_gate_up", "expert_w_down", "expert_b_down", "final_norm_g"]


def kernel(**inputs):
    import concourse.bacc as bacc
    from concourse.bass_utils import run_bass_kernel_spmd

    arrays = {n: np.ascontiguousarray(inputs[n]) for n in _DIRECT}
    arrays.update(constants())
    arrays["g_rows"] = np.concatenate([np.asarray(inputs[n]).reshape(KC, P)
                                       for n in ("mem_norm_g", "attn_norm_g", "ffn_norm_g")], 0)
    rpb = np.asarray(inputs["na_rpb"])[0]
    rows = np.zeros((NA_HEADS, REL), rpb.dtype)
    dc = np.arange(-(WIN_COLS - 1), WIN_COLS)
    for dr in range(-(S // GRID_W - 1), S // GRID_W):
        rows[:, GRID_W * dr + dc + S - 1] = rpb[:, dr + WIN_ROWS - 1, :]
    arrays["na_rows"] = rows
    nc = bacc.Bacc("TRN2", target_bir_lowering=False, num_devices=1)
    t = {n: nc.dram_tensor(f"in_{n}", a.shape, mybir.dt.from_np(a.dtype), kind="ExternalInput").ap()
         for n, a in arrays.items()}
    t["out"] = nc.dram_tensor("out_0", (1, S, D), F32, kind="ExternalOutput").ap()
    build(nc, t)
    r = run_bass_kernel_spmd(nc, [{f"in_{n}": a for n, a in arrays.items()}], core_ids=[0])
    return np.asarray(r.results[0]["out_0"])
```
